# Optimizing a Trainium2 kernel written in Bass

```python
import math
import jax, jax.numpy as jnp
from jax import lax
import numpy as np
import jax
import jax.numpy as jnp

D_MODEL = 1024
BATCH = 1
SEQ = 256
DEPTH = 1

D_RNN = D_MODEL
RNN_HEADS = 8
RNN_BLOCK = D_RNN // RNN_HEADS
RNN_CONV = 4
RG_C = 8.0
ATT_HEADS = 8
HEAD_DIM = 128
ATT_WIDTH = ATT_HEADS * HEAD_DIM
Q_BLOCK = 128
D_FF = 3 * D_MODEL
FFN_CONV = 3
EPS = 1e-6
IN_SPLITS = (D_RNN, D_RNN, ATT_WIDTH, ATT_WIDTH, ATT_WIDTH, D_MODEL, D_MODEL)
D_IN = sum(IN_SPLITS)


def rmsnorm(x, g):
    x32 = x.astype(jnp.float32)
    y = x32 * lax.rsqrt(jnp.mean(x32 * x32, axis=-1, keepdims=True) + EPS)
    return (y * g.astype(jnp.float32)).astype(x.dtype)

def causal_dwconv(x, w, b):
    k_w = w.shape[0]
    s = x.shape[1]
    xp = jnp.pad(x, ((0, 0), (k_w - 1, 0), (0, 0)))
    out = b + w[0] * xp[:, 0:s]
    for k in range(1, k_w):
        out = out + w[k] * xp[:, k:k + s]
    return out

def rg_lru(x, wa, ba, wx, bx, lam):
    b_, s_, c_ = x.shape
    xh = x.reshape(b_, s_, RNN_HEADS, RNN_BLOCK)
    r = jax.nn.sigmoid(jnp.einsum('bshi,hij->bshj', xh, wa).reshape(b_, s_, c_) + ba)
    i = jax.nn.sigmoid(jnp.einsum('bshi,hij->bshj', xh, wx).reshape(b_, s_, c_) + bx)
    log_a = -RG_C * r.astype(jnp.float32) * jax.nn.softplus(-lam.astype(jnp.float32))
    a = jnp.exp(log_a)
    mult = jnp.sqrt(-jnp.expm1(2.0 * log_a))
    u = mult * (i * x).astype(jnp.float32)

    def step(h, inp):
        a_t, u_t = inp
        h = a_t * h + u_t
        return h, h

    h0 = jnp.zeros((b_, c_), jnp.float32)
    _, hs = lax.scan(step, h0, (jnp.swapaxes(a, 0, 1), jnp.swapaxes(u, 0, 1)))
    return jnp.swapaxes(hs, 0, 1).astype(x.dtype)

def head_rmsnorm(x, g):
    return rmsnorm(x, g)

def stick_breaking_attention(q, k, v):
    b_, s_, h_, d_ = q.shape
    nb = s_ // Q_BLOCK
    scale = 1.0 / math.sqrt(d_)
    kh = jnp.transpose(k, (0, 2, 1, 3))
    vh = jnp.transpose(v, (0, 2, 1, 3))
    qb = jnp.transpose(q.reshape(b_, nb, Q_BLOCK, h_, d_), (1, 0, 3, 2, 4))
    key_pos = jnp.arange(s_)

    def one_block(args):
        q_blk, blk = args
        q_pos = blk * Q_BLOCK + jnp.arange(Q_BLOCK)
        mask = key_pos[None, :] < q_pos[:, None]
        z = jnp.einsum('bhqd,bhkd->bhqk', q_blk, kh).astype(jnp.float32) * scale
        log_beta = jax.nn.log_sigmoid(z)
        log_1mb = jnp.where(mask, log_beta - z, 0.0)
        suffix = lax.cumsum(log_1mb, axis=3, reverse=True) - log_1mb
        attn = jnp.where(mask, jnp.exp(log_beta + suffix), 0.0)
        return jnp.einsum('bhqk,bhkd->bhqd', attn.astype(v.dtype), vh)

    out = lax.map(one_block, (qb, jnp.arange(nb)))
    return jnp.transpose(out, (1, 0, 3, 2, 4)).reshape(b_, s_, h_ * d_)

def first_inputs(seed: int = 0) -> dict:
    key = jax.random.key(seed)
    ks = jax.random.split(key, 24)
    n = jax.random.normal
    L, D = DEPTH, D_MODEL
    u = jax.random.uniform(ks[10], (L, D_RNN), minval=0.9, maxval=0.999)
    a0 = u ** (1.0 / RG_C)
    lam = jnp.log(a0) - jnp.log1p(-a0)
    return {
        "x": n(ks[0], (BATCH, SEQ, D), jnp.float32),
        "c": n(ks[1], (BATCH, D), jnp.float32),
        "ada_w": n(ks[2], (L, D, 6 * D), jnp.float32) * (0.5 * D ** -0.5),
        "ada_b": n(ks[3], (L, 6 * D), jnp.float32) * 0.01,
        "norm1_g": 1.0 + 0.05 * n(ks[4], (L, D), jnp.float32),
        "w_in": n(ks[5], (L, D, D_IN), jnp.float32) * D ** -0.5,
        "conv_w": n(ks[6], (L, RNN_CONV, D_RNN), jnp.float32) * RNN_CONV ** -0.5,
        "conv_b": n(ks[7], (L, D_RNN), jnp.float32) * 0.01,
        "rg_wa": n(ks[8], (L, RNN_HEADS, RNN_BLOCK, RNN_BLOCK), jnp.float32) * RNN_BLOCK ** -0.5,
        "rg_ba": n(ks[9], (L, D_RNN), jnp.float32) * 0.01,
        "rg_wx": n(ks[11], (L, RNN_HEADS, RNN_BLOCK, RNN_BLOCK), jnp.float32) * RNN_BLOCK ** -0.5,
        "rg_bx": n(ks[12], (L, D_RNN), jnp.float32) * 0.01,
        "rg_lambda": lam.astype(jnp.float32),
        "q_norm_g": 1.0 + 0.05 * n(ks[13], (L, HEAD_DIM), jnp.float32),
        "k_norm_g": 1.0 + 0.05 * n(ks[14], (L, HEAD_DIM), jnp.float32),
        "w_out": n(ks[15], (L, D, D), jnp.float32) * D ** -0.5,
        "norm2_g": 1.0 + 0.05 * n(ks[16], (L, D), jnp.float32),
        "ffn_up": n(ks[17], (L, D, 2 * D_FF), jnp.float32) * D ** -0.5,
        "ffn_conv_w": n(ks[18], (L, FFN_CONV, 2 * D_FF), jnp.float32) * FFN_CONV ** -0.5,
        "ffn_conv_b": n(ks[19], (L, 2 * D_FF), jnp.float32) * 0.01,
        "ffn_down": n(ks[20], (L, D_FF, D), jnp.float32) * D_FF ** -0.5,
    }

def first_block(x, c, ada_w, ada_b, norm1_g, w_in, conv_w, conv_b, rg_wa, rg_ba, rg_wx, rg_bx,
              rg_lambda, q_norm_g, k_norm_g, w_out, norm2_g, ffn_up, ffn_conv_w, ffn_conv_b,
              ffn_down):
    b_, s_, d_ = x.shape
    cuts = np.cumsum(IN_SPLITS)[:-1].tolist()
    for l in range(DEPTH):
        mod = c @ ada_w[l] + ada_b[l]
        sh1, sc1, gt1, sh2, sc2, gt2 = [m[:, None, :] for m in jnp.split(mod, 6, axis=-1)]

        h = rmsnorm(x, norm1_g[l]) * (1.0 + sc1) + sh1
        p = h @ w_in[l]
        xr, yr, q, k, v, ga, gb = jnp.split(p, cuts, axis=-1)

        xr = causal_dwconv(xr, conv_w[l], conv_b[l])
        y_a = rg_lru(xr, rg_wa[l], rg_ba[l], rg_wx[l], rg_bx[l], rg_lambda[l]) * jax.nn.gelu(yr)

        q = head_rmsnorm(q.reshape(b_, s_, ATT_HEADS, HEAD_DIM), q_norm_g[l])
        k = head_rmsnorm(k.reshape(b_, s_, ATT_HEADS, HEAD_DIM), k_norm_g[l])
        v = v.reshape(b_, s_, ATT_HEADS, HEAD_DIM)
        y_b = stick_breaking_attention(q, k, v)

        mix = jax.nn.sigmoid(ga) * y_a + jax.nn.sigmoid(gb) * y_b
        x = x + gt1 * (mix @ w_out[l])

        h2 = rmsnorm(x, norm2_g[l]) * (1.0 + sc2) + sh2
        up = causal_dwconv(h2 @ ffn_up[l], ffn_conv_w[l], ffn_conv_b[l])
        g_ff, v_ff = jnp.split(up, 2, axis=-1)
        x = x + gt2 * ((jax.nn.gelu(g_ff) * v_ff) @ ffn_down[l])
    return x


MLA_HEADS = 8
MLA_Q_RANK = 256
MLA_KV_RANK = 128
MLA_NOPE = 64
MLA_ROPE = 32
MLA_V = 64
ROPE_THETA = 10000.0
DSA_HEADS = 8
DSA_KV_HEADS = 2
DSA_HEAD_DIM = 64
IDX_HEADS = 8
IDX_DIM = 32
IDX_TOPK_MAX = 256
N_EXPERTS = 32
TOP_K = 4
D_EXPERT = D_MODEL
SWIGLU_ALPHA = 1.702
SWIGLU_LIMIT = 7.0

NORM_EPS = 1e-6
NEG_INF = -1e30
MOE_BLOCK = 128

MIX_WIDTH = MLA_HEADS * MLA_V + DSA_HEADS * DSA_HEAD_DIM
IN_SPLITS_2 = (MLA_Q_RANK, MLA_KV_RANK, MLA_ROPE,
             DSA_HEADS * DSA_HEAD_DIM, DSA_KV_HEADS * DSA_HEAD_DIM, DSA_KV_HEADS * DSA_HEAD_DIM,
             IDX_HEADS * IDX_DIM, IDX_DIM, IDX_HEADS)
IN_WIDTH = sum(IN_SPLITS_2)


def rms_norm(x, g):
    xf = x.astype(jnp.float32)
    y = xf * lax.rsqrt(jnp.mean(xf * xf, axis=-1, keepdims=True) + NORM_EPS)
    return (y * g.astype(jnp.float32)).astype(x.dtype)

def rope(x, pos):
    half = x.shape[-1] // 2
    freqs = ROPE_THETA ** (-jnp.arange(half, dtype=jnp.float32) / half)
    ang = pos.astype(jnp.float32)[..., None] * freqs
    ang = ang.reshape(ang.shape[:2] + (1,) * (x.ndim - 3) + (half,))
    cos, sin = jnp.cos(ang), jnp.sin(ang)
    x1 = x[..., :half].astype(jnp.float32)
    x2 = x[..., half:].astype(jnp.float32)
    return jnp.concatenate([x1 * cos - x2 * sin, x2 * cos + x1 * sin], axis=-1).astype(x.dtype)

def to_blocks(a):
    b, s = a.shape[:2]
    return jnp.moveaxis(a.reshape((b, s // Q_BLOCK, Q_BLOCK) + a.shape[2:]), 1, 0)

def from_blocks(a):
    a = jnp.moveaxis(a, 0, 1)
    return a.reshape((a.shape[0], a.shape[1] * a.shape[2]) + a.shape[3:])

def mla_attention(c_q, c_kv, k_rope_in, pos, g_q_a, g_kv_a, w_q_b, w_kv_b):
    b, s, _ = c_q.shape
    q = (rms_norm(c_q, g_q_a) @ w_q_b).reshape(b, s, MLA_HEADS, MLA_NOPE + MLA_ROPE)
    q_nope = q[..., :MLA_NOPE]
    q_rope = rope(q[..., MLA_NOPE:], pos)
    kv = (rms_norm(c_kv, g_kv_a) @ w_kv_b).reshape(b, s, MLA_HEADS, MLA_NOPE + MLA_V)
    k_nope, v = kv[..., :MLA_NOPE], kv[..., MLA_NOPE:]
    k_rope = rope(k_rope_in, pos)
    scale = (MLA_NOPE + MLA_ROPE) ** -0.5
    key_idx = jnp.arange(s)

    def block(args):
        qn, qr, qi = args
        sc = (jnp.einsum('bqhd,bkhd->bhqk', qn, k_nope)
              + jnp.einsum('bqhd,bkd->bhqk', qr, k_rope)).astype(jnp.float32) * scale
        sc = jnp.where(key_idx[None, None, None, :] <= qi[None, None, :, None], sc, NEG_INF)
        p = jax.nn.softmax(sc, axis=-1).astype(v.dtype)
        return jnp.einsum('bhqk,bkhd->bqhd', p, v)

    q_ids = jnp.arange(s).reshape(-1, Q_BLOCK)
    out = lax.map(block, (to_blocks(q_nope), to_blocks(q_rope), q_ids))
    return from_blocks(out).reshape(b, s, MLA_HEADS * MLA_V)

def dsa_attention(q, k, v, q_i, k_i, w_i, pos):
    b, s, _ = q.shape
    grp = DSA_HEADS // DSA_KV_HEADS
    q = q.reshape(b, s, DSA_KV_HEADS, grp, DSA_HEAD_DIM)
    k = k.reshape(b, s, DSA_KV_HEADS, DSA_HEAD_DIM)
    v = v.reshape(b, s, DSA_KV_HEADS, DSA_HEAD_DIM)
    q_i = q_i.reshape(b, s, IDX_HEADS, IDX_DIM) * (IDX_DIM ** -0.5)
    w_i = w_i * (IDX_HEADS ** -0.5)
    n_sel = min(IDX_TOPK_MAX, s // 4)
    key_idx = jnp.arange(s)
    slopes = jnp.exp2(-8.0 * jnp.arange(1, DSA_HEADS + 1, dtype=jnp.float32) / DSA_HEADS)
    slopes = slopes.reshape(DSA_KV_HEADS, grp)
    gather = jax.vmap(lambda a, i: a[i])

    def block(args):
        qb, qib, wib, posb, ti = args
        rel = jax.nn.relu(jnp.einsum('bqhd,bsd->bqsh', qib, k_i).astype(jnp.float32))
        idx_score = jnp.einsum('bqsh,bqh->bqs', rel, wib.astype(jnp.float32))
        idx_score = jnp.where(key_idx[None, None, :] <= ti[None, :, None], idx_score, NEG_INF)
        _, sel = lax.top_k(idx_score, n_sel)
        k_sel = gather(k, sel)
        v_sel = gather(v, sel)
        pos_sel = gather(pos, sel)
        sc = jnp.einsum('bqhgd,bqnhd->bqhgn', qb, k_sel).astype(jnp.float32) * (DSA_HEAD_DIM ** -0.5)
        dist = jnp.abs(posb[:, :, None] - pos_sel).astype(jnp.float32)
        sc = sc - slopes[None, None, :, :, None] * dist[:, :, None, None, :]
        valid = sel <= ti[None, :, None]
        sc = jnp.where(valid[:, :, None, None, :], sc, NEG_INF)
        p = jax.nn.softmax(sc, axis=-1).astype(v.dtype)
        return jnp.einsum('bqhgn,bqnhd->bqhgd', p, v_sel)

    q_ids = jnp.arange(s).reshape(-1, Q_BLOCK)
    out = lax.map(block, (to_blocks(q), to_blocks(q_i), to_blocks(w_i), to_blocks(pos), q_ids))
    return from_blocks(out).reshape(b, s, DSA_HEADS * DSA_HEAD_DIM)

def moe_ffn(h, w_router, b_router, w_mlp1, b_mlp1, w_mlp2, b_mlp2):
    b, s, d = h.shape
    xf = h.reshape(-1, d)
    n = xf.shape[0]
    logits = (xf @ w_router + b_router).astype(jnp.float32)
    top_val, top_idx = lax.top_k(logits, TOP_K)
    gates = jax.nn.softmax(top_val, axis=-1)
    n_assign = n * TOP_K
    flat_e = top_idx.reshape(-1)
    flat_tok = jnp.arange(n_assign, dtype=jnp.int32) // TOP_K
    flat_gate = gates.reshape(-1)
    order = jnp.argsort(flat_e)
    e_sorted = flat_e[order]
    counts = jnp.bincount(flat_e, length=N_EXPERTS)
    start = jnp.cumsum(counts) - counts
    padded = (counts + MOE_BLOCK - 1) // MOE_BLOCK * MOE_BLOCK
    pad_end = jnp.cumsum(padded)
    pad_start = pad_end - padded
    dest = pad_start[e_sorted] + jnp.arange(n_assign) - start[e_sorted]
    n_slots = (n_assign + MOE_BLOCK - 1) // MOE_BLOCK * MOE_BLOCK + N_EXPERTS * MOE_BLOCK
    n_blocks = n_slots // MOE_BLOCK
    slot_tok = jnp.full((n_slots,), n, jnp.int32).at[dest].set(flat_tok[order])
    slot_gate = jnp.zeros((n_slots,), jnp.float32).at[dest].set(flat_gate[order])
    block_e = jnp.minimum(
        jnp.searchsorted(pad_end, jnp.arange(n_blocks) * MOE_BLOCK, side='right'), N_EXPERTS - 1)
    x_pad = jnp.concatenate([xf, jnp.zeros((1, d), xf.dtype)], axis=0)
    x_slots = x_pad[slot_tok].reshape(n_blocks, MOE_BLOCK, d)

    def expert_block(args):
        xb, e = args
        hid = xb @ w_mlp1[e] + b_mlp1[e]
        glu = jnp.minimum(hid[..., ::2], SWIGLU_LIMIT)
        lin = jnp.clip(hid[..., 1::2], -SWIGLU_LIMIT, SWIGLU_LIMIT)
        act = glu * jax.nn.sigmoid(SWIGLU_ALPHA * glu) * (lin + 1.0)
        return act @ w_mlp2[e] + b_mlp2[e]

    y = lax.map(expert_block, (x_slots, block_e)).reshape(n_slots, d)
    y = y * slot_gate[:, None].astype(y.dtype)
    out = jax.ops.segment_sum(y, slot_tok, num_segments=n + 1)[:n]
    return out.reshape(b, s, d)

def second_inputs(seed: int = 0) -> dict:
    key = jax.random.key(seed)
    ks = jax.random.split(key, 24)
    f32 = jnp.float32
    L, D, F, E = DEPTH, D_MODEL, D_EXPERT, N_EXPERTS

    def nrm(k, shape, scale):
        return jax.random.normal(k, shape, f32) * scale

    def gain(k, width):
        return 1.0 + nrm(k, (L, width), 0.02)

    x = nrm(ks[0], (BATCH, SEQ, D), 1.0)
    c = nrm(ks[1], (BATCH, D), 1.0)
    offsets = jax.random.randint(ks[2], (BATCH, 1), 0, 4096, dtype=jnp.int32)
    positions = offsets + jnp.arange(SEQ, dtype=jnp.int32)[None, :]
    return {
        "x": x,
        "c": c,
        "positions": positions,
        "w_ada": nrm(ks[3], (L, D, 6 * D), 0.2 * D ** -0.5),
        "b_ada": nrm(ks[4], (L, 6 * D), 0.01),
        "g_pre_mix": gain(ks[5], D),
        "g_post_mix": gain(ks[6], D),
        "g_pre_ffn": gain(ks[7], D),
        "g_post_ffn": gain(ks[8], D),
        "w_in": nrm(ks[9], (L, D, IN_WIDTH), D ** -0.5),
        "g_q_a": gain(ks[10], MLA_Q_RANK),
        "g_kv_a": gain(ks[11], MLA_KV_RANK),
        "w_q_b": nrm(ks[12], (L, MLA_Q_RANK, MLA_HEADS * (MLA_NOPE + MLA_ROPE)), MLA_Q_RANK ** -0.5),
        "w_kv_b": nrm(ks[13], (L, MLA_KV_RANK, MLA_HEADS * (MLA_NOPE + MLA_V)), MLA_KV_RANK ** -0.5),
        "w_o": nrm(ks[14], (L, MIX_WIDTH, D), MIX_WIDTH ** -0.5),
        "w_router": nrm(ks[15], (L, D, E), D ** -0.5),
        "b_router": nrm(ks[16], (L, E), 0.01),
        "w_mlp1": nrm(ks[17], (L, E, D, 2 * F), D ** -0.5),
        "b_mlp1": nrm(ks[18], (L, E, 2 * F), 0.01),
        "w_mlp2": nrm(ks[19], (L, E, F, D), F ** -0.5),
        "b_mlp2": nrm(ks[20], (L, E, D), 0.01),
    }

def second_block(x, c, positions, w_ada, b_ada, g_pre_mix, g_post_mix, g_pre_ffn, g_post_ffn,
              w_in, g_q_a, g_kv_a, w_q_b, w_kv_b, w_o, w_router, b_router,
              w_mlp1, b_mlp1, w_mlp2, b_mlp2):
    split_at = np.cumsum(IN_SPLITS_2)[:-1].tolist()
    cond = jax.nn.silu(c)
    for l in range(DEPTH):
        mod = cond @ w_ada[l] + b_ada[l]
        sh1, sc1, gt1, sh2, sc2, gt2 = [m[:, None, :] for m in jnp.split(mod, 6, axis=-1)]

        h = rms_norm(x, g_pre_mix[l]) * (1.0 + sc1) + sh1
        proj = h @ w_in[l]
        (c_q, c_kv, k_rope, q_d, k_d, v_d, q_idx, k_idx, w_idx) = jnp.split(proj, split_at, axis=-1)
        y_mla = mla_attention(c_q, c_kv, k_rope, positions, g_q_a[l], g_kv_a[l], w_q_b[l], w_kv_b[l])
        y_dsa = dsa_attention(q_d, k_d, v_d, q_idx, k_idx, w_idx, positions)
        mix = jnp.concatenate([y_mla, y_dsa], axis=-1) @ w_o[l]
        x = x + gt1 * rms_norm(mix, g_post_mix[l])

        h2 = rms_norm(x, g_pre_ffn[l]) * (1.0 + sc2) + sh2
        ffn = moe_ffn(h2, w_router[l], b_router[l], w_mlp1[l], b_mlp1[l], w_mlp2[l], b_mlp2[l])
        x = x + gt2 * rms_norm(ffn, g_post_ffn[l])
    return x


def setup_inputs(seed=0):
    out = dict(first_inputs(seed))
    for name, value in second_inputs(seed + 1).items():
        if name != "x":
            out[name + "_2"] = value
    return out


def reference(
    x, c, ada_w, ada_b, norm1_g, w_in, conv_w, conv_b, rg_wa, rg_ba, rg_wx, rg_bx, rg_lambda,
    q_norm_g, k_norm_g, w_out, norm2_g, ffn_up, ffn_conv_w, ffn_conv_b, ffn_down, c_2,
    positions_2, w_ada_2, b_ada_2, g_pre_mix_2, g_post_mix_2, g_pre_ffn_2, g_post_ffn_2, w_in_2,
    g_q_a_2, g_kv_a_2, w_q_b_2, w_kv_b_2, w_o_2, w_router_2, b_router_2, w_mlp1_2, b_mlp1_2,
    w_mlp2_2, b_mlp2_2,
):
    x = first_block(
        x, c, ada_w, ada_b, norm1_g, w_in, conv_w, conv_b, rg_wa, rg_ba, rg_wx, rg_bx,
        rg_lambda, q_norm_g, k_norm_g, w_out, norm2_g, ffn_up, ffn_conv_w, ffn_conv_b, ffn_down,
    )
    return second_block(
        x, c_2, positions_2, w_ada_2, b_ada_2, g_pre_mix_2, g_post_mix_2, g_pre_ffn_2,
        g_post_ffn_2, w_in_2, g_q_a_2, g_kv_a_2, w_q_b_2, w_kv_b_2, w_o_2, w_router_2,
        b_router_2, w_mlp1_2, b_mlp1_2, w_mlp2_2, b_mlp2_2,
    )


_drawn_inputs = setup_inputs


def setup_inputs(seed=0):
    import zlib

    import numpy as np

    out = dict(_drawn_inputs(seed))
    spreads = {}
    factors = {'conv_b': 4.135,
     'rg_ba': 8.0,
     'rg_bx': 8.0,
     'q_norm_g': 5.075,
     'k_norm_g': 5.896,
     'ffn_conv_b': 4.924,
     'b_ada_2': 3.201,
     'g_pre_mix_2': 4.492,
     'g_post_mix_2': 22.261,
     'g_pre_ffn_2': 5.279,
     'g_post_ffn_2': 43.564,
     'g_q_a_2': 8.0,
     'g_kv_a_2': 8.0,
     'b_router_2': 8.0,
     'b_mlp1_2': 37.399,
     'b_mlp2_2': 64.0}
    for name, (base, spread) in spreads.items():
        noise = np.random.default_rng([zlib.crc32(name.encode()), seed]).standard_normal(out[name].shape)
        drawn = base * np.exp(spread * noise) if base else spread * noise
        out[name] = jnp.asarray(drawn.astype(out[name].dtype))
    for name, factor in factors.items():
        out[name] = (out[name] * factor).astype(out[name].dtype)
    return out
```

```python
from contextlib import ExitStack

import numpy as np

import concourse.bass as bass
from concourse import mybir

F32 = mybir.dt.float32
BF16 = mybir.dt.bfloat16
I32 = mybir.dt.int32
ALU = mybir.AluOpType
ACT = mybir.ActivationFunctionType
AX = mybir.AxisListType

S = 256
D = 1024
NK = 8
EPS = 1e-6
NEG = -1e30
NE = 32
CAP = 64
RING = 15
SLOT = 2048

COLS = {}


def _layout_cols():
    n = 0
    for name, w in (("c", 8), ("c2", 8), ("ada_b", 48), ("b_ada2", 48), ("norm1", 8), ("norm2", 8),
                    ("conv_w", 32), ("conv_b", 8), ("ba", 8), ("bx", 8), ("lam", 8), ("qg", 1), ("kg", 1),
                    ("fw", 144), ("fb", 48), ("pre_mix", 8), ("post_mix", 8), ("pre_ffn", 8),
                    ("post_ffn", 8), ("gq", 2), ("gkv", 1)):
        COLS[name] = (n, w)
        n += w
    return n


NCOL = _layout_cols()

CONST = {}


def _layout_consts():
    n = 0
    for name, w in (("ident", 128), ("ones", 128), ("nones", 128), ("negU", 128), ("uinc", 128), ("smask", 384),
                    ("sbias", 384), ("cbias", 384), ("iota", 256), ("freq", 1), ("sign", 1)):
        CONST[name] = (n, w)
        n += w
    return n


NCONST = _layout_consts()


def constants():
    c = np.zeros((128, NCONST), np.float32)

    def put(name, v):
        o, w = CONST[name]
        c[:, o:o + w] = v

    p = np.arange(128)[:, None]
    f = np.arange(128)[None, :]
    put("ident", (p == f).astype(np.float32))
    put("ones", 1.0)
    put("nones", -1.0)
    put("negU", -(p >= f).astype(np.float32))
    put("uinc", (p <= f).astype(np.float32))
    strict = (p < f).astype(np.float32)
    one = np.ones((128, 128), np.float32)
    m = np.concatenate([strict, one, strict], 1)
    put("smask", m)
    put("sbias", np.where(m > 0, 0.0, NEG))
    tri = np.where(f <= p, 0.0, NEG)
    put("cbias", np.concatenate([tri, 0 * one, tri], 1))
    put("iota", np.concatenate([f % 64, 64 + f % 64], 1).astype(np.float32) * np.ones((128, 1)))
    half = 16
    fr = np.float32(10000.0) ** (-np.arange(half, dtype=np.float32) / np.float32(half))
    put("freq", fr[p % half].astype(np.float32))
    put("sign", np.where((p % 32) < 16, -1.0, 1.0))
    return c


def two_pi_parts():
    rest = 2.0 * np.pi
    parts = []
    for _ in range(4):
        e = np.floor(np.log2(rest))
        q = 2.0 ** (e - 11)
        v = np.floor(rest / q) * q
        parts.append(float(v))
        rest -= v
    return parts


class Prog:

    ENGINES = ("pe", "act", "dve", "pool", "sp")

    def __init__(self, me, eng, semaphore):
        self.me, self.eng, self.semaphore = me, eng, semaphore
        self.new_semaphores("")

    def new_semaphores(self, suffix):
        self.sem = {e: self.semaphore("s_" + e + suffix) for e in self.ENGINES}
        self.restart()

    def restart(self):
        self.cnt = {e: 0 for e in self.ENGINES}
        self.seen = {}

    def wait(self, eng, *tokens):
        if eng != self.me:
            return
        for t in _flat(tokens):
            sem, val = (self.sem[t[0]], t[1]) if isinstance(t[0], str) else t
            if self.seen.get(id(sem), 0) < val:
                self.seen[id(sem)] = val
                self.eng.wait_ge(sem, val)

    def op(self, eng, fn, *tokens, inc=True):
        self.wait(eng, *tokens)
        if inc:
            self.cnt[eng] += 1
        if eng == self.me:
            made = fn(self.eng)
            if inc:
                made.then_inc(self.sem[eng], 1)
        return (eng, self.cnt[eng]) if inc else None

    def dma(self, eng, fn, sem, *tokens):
        self.wait(eng, *tokens)
        if eng == self.me:
            fn(self.eng).then_inc(sem, 16)

    def last(self, eng):
        return (eng, self.cnt[eng]) if self.cnt[eng] else None

    def begin_if(self, engines, taken):
        self.engines, self.before, self.saw = engines, dict(self.cnt), dict(self.seen)
        self.branch = ExitStack()
        if self.me in engines:
            self.branch.enter_context(self.eng.If(taken))
        self.full = None

    def begin_else(self):
        self.branch.close()
        self.full = self.cnt
        self.cnt, self.seen = dict(self.before), dict(self.saw)
        self.branch = ExitStack()
        if self.me in self.engines:
            self.branch.enter_context(self.eng.Else())

    def end_if(self):
        if self.full is None:
            self.begin_else()
        if self.me in self.engines and self.full[self.me] > self.cnt[self.me]:
            self.eng.wait_ge(self.sem[self.me], self.cnt[self.me])
            self.eng.sem_inc(self.sem[self.me], self.full[self.me] - self.cnt[self.me])
        self.branch.close()
        self.cnt, self.seen = self.full, self.saw

    def begin_loop(self, engines, load):
        self.restart()
        self.rounds = ExitStack()
        if self.me in engines:
            self.rounds.enter_context(self.eng.While(lambda: load(self.eng) > 0))

    def end_loop(self, load, clear, bar, go, again):
        if self.me == "sp":
            self.eng.wait_ge(bar, len(go))
            for s in clear:
                self.eng.sem_clear(s)
            self.eng.sem_clear(bar)
            with self.eng.If(load(self.eng) > 0):
                for dst, src, sem in again:
                    self.eng.dma_start(dst, src).then_inc(sem, 16)
            for s in go.values():
                self.eng.sem_inc(s, 1)
        elif self.me in go:
            self.eng.wait_ge(self.sem[self.me], self.cnt[self.me])
            self.eng.sem_inc(bar, 1)
            self.eng.wait_ge(go[self.me], 1)
            self.eng.sem_clear(go[self.me])
        self.rounds.close()
        self.restart()


def _flat(x):
    for t in x:
        if t is None:
            continue
        if isinstance(t, tuple):
            yield t
        else:
            yield from _flat(t)


def program(nc, a, out, stage=99):
    with ExitStack() as ctx:
        made = {}

        def sb(name, shape, dt=F32):
            if name not in made:
                made[name] = ctx.enter_context(nc.sbuf_tensor(name, shape, dt))
            return made[name]

        def psum(name):
            if name not in made:
                made[name] = ctx.enter_context(nc.psum_tensor(name, [128, 512], F32))
            return made[name]

        def sem(name):
            if name not in made:
                made[name] = ctx.enter_context(nc.semaphore(name))
            return made[name]

        walk(None, None, a, out, sb, psum, sem)
        block = ctx.enter_context(nc.Block())
        block.sync(lambda e: walk("sp", e, a, out, sb, psum, sem))
        block.tensor(lambda e: walk("pe", e, a, out, sb, psum, sem))
        block.scalar(lambda e: walk("act", e, a, out, sb, psum, sem))
        block.vector(lambda e: walk("dve", e, a, out, sb, psum, sem))
        block.gpsimd(lambda e: walk("pool", e, a, out, sb, psum, sem))


def walk(me, eng, a, out, sb, psum, sem):
        P = Prog(me, eng, sem)

        serial = [False]

        def V(fn, *w):
            return P.op("dve", fn, P.last("dve") if serial[0] else None, *w)

        def A(fn, *w):
            return P.op("act", fn, *w)

        def G(fn, *w):
            return P.op("pool", fn, *w)

        def T(fn, *w, inc=False):
            return P.op("pe", fn, *w, inc=inc)

        ring = sb("ring", [128, RING, SLOT])
        con = sb("con", [128, NCONST])
        col = sb("col", [128, NCOL])
        modc = sb("modc", [128, 2, 48])
        mc = sb("mc", [128, 48])
        xT = sb("xT", [128, 8, 256])
        hT = sb("hT", [128, 8, 256])
        SCN = 14700
        scr = sb("scr", [128, SCN])
        B = [psum(f"bank{i}") for i in range(8)]

        def K(name, a0=0, a1=None):
            o, w = CONST[name]
            return con[:, o + a0:o + (w if a1 is None else a1)]

        def C(name, i=0, n=1):
            o, w = COLS[name]
            return col[:, o + i:o + i + n]

        used = [0]

        def carve(*dims):
            n = int(np.prod(dims))
            o = used[0]
            used[0] += n
            assert used[0] <= SCN, used[0]
            v = scr[:, o:o + n]
            if len(dims) == 2:
                v = v.rearrange("p (a b) -> p a b", a=dims[0])
            if len(dims) == 3:
                v = v.rearrange("p (a b c) -> p a b c", a=dims[0], b=dims[1])
            return v

        def fence():
            every = [P.last(e) for e in ("pe", "act", "dve", "pool")]
            for e in ("pe", "act", "dve", "pool"):
                P.wait(e, *every)
            used[0] = 0

        freed = {i: None for i in range(8)}
        turn = [0]
        pool_banks = [list(range(8))]

        def bank():
            lst = pool_banks[0]
            i = lst[turn[0] % len(lst)]
            turn[0] += 1
            return i, B[i], freed[i]

        slot_sem = [sem(f"w{i}") for i in range(RING)]
        slot_use = [0] * RING
        slot_free = [None] * RING
        piece = [0]

        def slot_view(s, src, n):
            dst = ring[0:src.shape[0], s, 0:n]
            if len(src.shape) == 3:
                dst = dst.rearrange("p (a b) -> p a b", a=src.shape[1])
            return dst

        def load(src, n=SLOT):
            s = piece[0] % RING
            piece[0] += 1
            assert slot_free[s] is not False
            slot_use[s] += 16
            dst = slot_view(s, src, n)
            P.dma("sp", lambda e: e.dma_start(dst, src), slot_sem[s], slot_free[s])
            slot_free[s] = False
            return s, ring[:, s, 0:n], (slot_sem[s], slot_use[s])

        def done(s, token):
            slot_free[s] = token

        s_small = [sem(f"small{i}") for i in range(8)]
        P.dma("act", lambda e: e.dma_start(col[:, :], a["cols"]), s_small[0])
        P.dma("act", lambda e: e.dma_start(con[:, :], a["consts"]), s_small[1])
        P.dma("act", lambda e: e.dma_start(xT[:, :, :], a["xT"]), s_small[2])
        t_col, t_con, t_x = (s_small[0], 16), (s_small[1], 16), (s_small[2], 16)

        eps = sb("eps", [128, 1])
        onec = sb("onec", [128, 1])
        t_eps = V(lambda e: e.memset(eps[:, :], EPS))
        t_eps = V(lambda e: e.memset(onec[:, :], 1.0))
        t_eps = [t_eps, ("dve", 1)]

        def rms(src, n, dim, sq, rst, width, *w):
            flat = src.rearrange("p a b -> p (a b)") if n > 1 else src
            sqf = sq.rearrange("p a b -> p (a b)") if n > 1 else sq
            t = A(lambda e: e.activation(sqf, flat, ACT.Square), *w)
            i, b, fr = bank()
            for k in range(n):
                rk = sq[:, k, :] if n > 1 else sq
                tt = T(lambda e, k=k, rk=rk: e.matmul(b[:, 0:width], K("ones"), rk, start=(k == 0), stop=(k == n - 1)),
                       t, fr, t_con, inc=(k == n - 1))
            t = A(lambda e: e.activation(rst, b[:, 0:width], ACT.Sqrt, bias=eps[:, 0:1], scale=1.0 / dim), tt, t_eps)
            freed[i] = t
            return V(lambda e: e.reciprocal(rst, rst), t)

        crep = sb("crep", [128, 8, 32])
        rowsb = sb("rowsb", [128, 512])
        t_rows = [None]

        def make_crep(src, *w):
            v = None
            for k in range(8):
                v = V(lambda e, k=k: e.tensor_scalar(crep[:, k, :], K("ones", 0, 32), src[:, k:k + 1], None, ALU.mult),
                      t_con, t_col, P.last("pe"), *w)
            return v

        def ada(w_dram, g, blk, bias, t_c):
            i, b, fr = bank()
            for k in range(8):
                s, v, tl = load(w_dram[k * 128:(k + 1) * 128, g * 2048:(g + 1) * 2048])
                for j in range(4):
                    t = T(lambda e, k=k, j=j, v=v: e.matmul(b[32 * j:32 * j + 32, :], crep[:, k, :],
                                                            v[:, 512 * j:512 * j + 512], start=(k == 0), stop=(k == 7)),
                          tl, fr, t_c, inc=(j == 3))
                done(s, t)
            t = A(lambda e: e.activation(rowsb[:, :], b[:, :], ACT.Copy), t, t_rows[0])
            freed[i] = t
            i, b2, fr = bank()
            for q in range(4):
                tt = T(lambda e, q=q: e.transpose(b2[:, q * 128:(q + 1) * 128], rowsb[:, q * 128:(q + 1) * 128],
                                                  K("ident")), t, fr, inc=(q == 3))
            t_rows[0] = tt
            src = b2[:, :].rearrange("p (b j r) -> p b j r", b=4, r=32)[:, :, :, 0]
            dst = modc[:, blk, g * 16:g * 16 + 16].rearrange("p (j b) -> p b j", b=4)
            t = V(lambda e: e.tensor_copy(dst, src), tt)
            freed[i] = t
            return V(lambda e: e.tensor_tensor(modc[:, blk, g * 16:g * 16 + 16], modc[:, blk, g * 16:g * 16 + 16],
                                               C(bias, g * 16, 16), ALU.add), t, t_col)

        def modulate(blk, which, gname, rst, tmp, *w):
            sh, sc = which * 8, which * 8 + 8
            t1 = V(lambda e: e.scalar_tensor_tensor(mc[:, 0:8], modc[:, blk, sc:sc + 8], 1.0, C(gname, 0, 8), ALU.add,
                                                    ALU.mult), *w)
            t2 = V(lambda e: e.tensor_tensor(tmp, xT[:, :, :], rst.unsqueeze(1).to_broadcast([128, 8, 256]), ALU.mult),
                   *w)
            o = []
            for k in range(8):
                if k % 2:
                    o.append(V(lambda e, k=k: e.tensor_scalar(hT[:, k, :], tmp[:, k, :], mc[:, k:k + 1],
                                                              modc[:, blk, sh + k:sh + k + 1], ALU.mult, ALU.add),
                               t1, t2))
                else:
                    o.append(A(lambda e, k=k: e.activation(hT[:, k, :], tmp[:, k, :], ACT.Identity,
                                                           bias=modc[:, blk, sh + k:sh + k + 1],
                                                           scale=mc[:, k:k + 1]), t1, t2))
            return o

        def tiles2(v, rhs, w, kn=8, b=None, fr=None):
            for j in range(2):
                for k in range(kn):
                    t = T(lambda e, j=j, k=k: e.matmul(b[:, 256 * j:256 * j + 256],
                                                       v[:, k * 256 + j * 128:k * 256 + j * 128 + 128],
                                                       rhs[:, k, :], start=(k == 0), stop=(k == kn - 1)),
                          fr, w, inc=(j == 1 and k == kn - 1))
            return t

        t_c = make_crep(C("c", 0, 8))
        sq = carve(8, 256)
        rst = carve(256)
        t_r = rms(xT[:, :, :], 8, D, sq, rst, 256, t_x)
        t_m = ada(a["ada_w"], 0, 0, "ada_b", t_c)
        t_h = modulate(0, 0, "norm1", rst, sq, t_m, t_r)
        fence()

        qk = [carve(8, 256), carve(8, 256)]
        vv = carve(2, 1024)
        mix = carve(8, 256)
        Wt = [carve(512) for _ in range(10)]
        rstq = carve(512)
        xp = carve(2, 260)

        def w_in(ci):
            s, v, tl = load(a["w_in"][ci])
            return s, v, tl

        def t_tile_chunk(ci):
            s, v, tl = w_in(ci)
            i, b, fr = bank()
            t = tiles2(v, hT, [tl, t_h], b=b, fr=fr)
            done(s, t)
            return i, b, t

        for which, base, g in ((0, 8, "qg"), (1, 12, "kg")):
            for c in range(4):
                i, b, t = t_tile_chunk(base + c)
                dst = qk[which][:, 2 * c:2 * c + 2, :].rearrange("p a b -> p (a b)")
                t1 = V(lambda e: e.tensor_copy(dst, b[:, :]), t)
                freed[i] = t1
                t2 = rms(dst, 1, 128, Wt[0], rstq, 512, t1, P.last("dve"), P.last("pe"))
                t3 = V(lambda e, dst=dst, g=g: e.scalar_tensor_tensor(dst, dst, C(g), rstq, ALU.mult, ALU.mult),
                       t1, t2)
                if which == 0:
                    t3 = V(lambda e, dst=dst: e.tensor_scalar(dst, dst, 128.0 ** -0.5, None, ALU.mult), t3)
                if which == 0:
                    t_q = t3
                t_k = t3
        for c in range(4):
            s, v, tl = w_in(16 + c)
            i, b, fr = bank()
            for tt in range(2):
                for k in range(8):
                    t = T(lambda e, tt=tt, k=k: e.matmul(b[:, 256 * tt:256 * tt + 256],
                                                         hT[:, k, tt * 128:(tt + 1) * 128],
                                                         v[:, k * 256:(k + 1) * 256], start=(k == 0), stop=(k == 7)),
                          fr, tl, t_h, inc=(tt == 1 and k == 7))
            done(s, t)
            t_v = A(lambda e, c=c: e.activation(vv[:, :, 256 * c:256 * c + 256],
                                                b[:, :].rearrange("p (a b) -> p a b", a=2), ACT.Copy), t)
            freed[i] = t_v

        lt = [carve(8) for _ in range(6)]
        t = A(lambda e: e.activation(lt[0], C("lam", 0, 8), ACT.Abs), t_col)
        t = A(lambda e: e.activation(lt[0], lt[0], ACT.Exp, scale=-1.0), t)
        t = V(lambda e: e.tensor_scalar(lt[1], lt[0], 2.0, None, ALU.add), t)
        t = V(lambda e: e.reciprocal(lt[1], lt[1]), t)
        t = V(lambda e: e.tensor_tensor(lt[1], lt[1], lt[0], ALU.mult), t)
        t = V(lambda e: e.tensor_tensor(lt[2], lt[1], lt[1], ALU.mult), t)
        t = V(lambda e: e.tensor_scalar(lt[3], lt[2], 1.0 / 19.0, 1.0 / 17.0, ALU.mult, ALU.add), t)
        for n in range(15, 0, -2):
            t = V(lambda e: e.tensor_tensor(lt[3], lt[3], lt[2], ALU.mult), t)
            t = V(lambda e, n=n: e.tensor_scalar(lt[3], lt[3], 1.0 / n, None, ALU.add), t)
        t = V(lambda e: e.scalar_tensor_tensor(lt[3], lt[3], 2.0, lt[1], ALU.mult, ALU.mult), t)
        t = V(lambda e: e.tensor_scalar(lt[4], C("lam", 0, 8), -1.0, 0.0, ALU.mult, ALU.max), t)
        t = V(lambda e: e.tensor_tensor(lt[3], lt[3], lt[4], ALU.add), t)
        sp8 = sb("sp8", [128, 16])
        t_sp = V(lambda e: e.tensor_scalar(sp8[:, 0:8], lt[3], 8.0, None, ALU.mult), t)
        t_sp = V(lambda e: e.tensor_scalar(sp8[:, 8:16], lt[3], -8.0, None, ALU.mult), t)
        hb = sb("hb", [128, 16])
        t_hb = V(lambda e: e.tensor_scalar(hb[:, 0:8], C("ba", 0, 8), 0.5, None, ALU.mult), t_col)
        t_hb = V(lambda e: e.tensor_scalar(hb[:, 8:16], C("bx", 0, 8), 0.5, None, ALU.mult), t_col)

        s_rg, rg, t_rg = load(a["rg"])
        t_pad = V(lambda e: e.memset(xp[:, :, 0:3], 0.0))

        att = {}

        def att1(h):
            i, b, fr = bank()
            q, k = qk[0][:, h, :], qk[1][:, h, :]
            T(lambda e: e.matmul(b[:, 0:256], k[:, 0:128], q, start=True, stop=False, skip_group_check=True),
              fr, t_q, t_k)
            t = T(lambda e: e.matmul(b[:, 256:384], k[:, 128:256], q[:, 128:256], start=False, stop=False,
                                     skip_group_check=True), inc=True)
            w0, w1 = Wt[8][:, 0:384], Wt[9][:, 0:384]
            t1 = A(lambda e: e.activation(w0, b[:, 0:384], ACT.Abs), t, P.last("dve"), P.last("pe"))
            t1 = A(lambda e: e.activation(w0, w0, ACT.Exp, scale=-1.0), t1)
            t1 = A(lambda e: e.activation(w0, w0, ACT.Ln, bias=onec[:, 0:1]), t1)
            t1 = V(lambda e: e.scalar_tensor_tensor(w1, b[:, 0:384], 0.0, w0, ALU.max, ALU.add), t1, P.last("pe"))
            t1 = V(lambda e: e.tensor_tensor(w1, w1, K("smask"), ALU.mult), t1)
            att[h] = (i, b, t1)

        def att2(h):
            i, b, t1 = att[h]
            w0, w1 = Wt[8][:, 0:384], Wt[9][:, 0:384]
            T(lambda e: e.matmul(b[:, 0:384], K("negU"), w1, start=False, stop=False, skip_group_check=True), t1)
            t = T(lambda e: e.matmul(b[:, 128:256], K("nones"), w1[:, 256:384], start=False, stop=True,
                                     skip_group_check=True), inc=True)
            t1 = V(lambda e: e.tensor_tensor(w0, b[:, 0:384], K("sbias"), ALU.add), t, P.last("act"))
            freed[i] = t1
            t1 = A(lambda e: e.activation(w0, w0, ACT.Exp), t1)
            att[h] = t1

        def att3(h):
            w0 = Wt[8][:, 0:384]
            i, b, fr = bank()
            T(lambda e: e.matmul(b[:, 0:256], vv[:, 0, h * 128:(h + 1) * 128], w0[:, 0:256], start=True, stop=False,
                                 skip_group_check=True), fr, att[h], t_v)
            t = T(lambda e: e.matmul(b[:, 128:256], vv[:, 1, h * 128:(h + 1) * 128], w0[:, 256:384], start=False,
                                     stop=True, skip_group_check=True), inc=True)
            t1 = V(lambda e: e.tensor_copy(qk[0][:, h, :], b[:, 0:256]), t)
            freed[i] = t1
            att[h] = t1

        def step(n):
            if n % 2 == 0:
                if n >= 2:
                    att3(n // 2 - 1)
                if n < 16:
                    att1(n // 2)
            else:
                att2(n // 2)

        def mixv(c):
            return mix[:, 2 * c:2 * c + 2, :].rearrange("p a b -> p (a b)")

        nstep = 0
        t_mix = {}
        for c in range(4):
            i, b, t = t_tile_chunk(c)
            step(nstep)
            nstep += 1
            t1 = A(lambda e: e.activation(xp[:, :, 3:259], b[:, :].rearrange("p (a b) -> p a b", a=2), ACT.Copy), t,
                   t_pad, P.last("dve"))
            freed[i] = t1
            for j in range(2):
                tl_ = 2 * c + j
                xc = Wt[0][:, 256 * j:256 * j + 256]
                t2 = V(lambda e, j=j, xc=xc, tl_=tl_: e.tensor_scalar(xc, xp[:, j, 3:259], C("conv_w", 24 + tl_),
                                                                      C("conv_b", tl_), ALU.mult, ALU.add),
                       t1, P.last("pe"))
                for k in (2, 1, 0):
                    t2 = V(lambda e, j=j, xc=xc, tl_=tl_, k=k: e.scalar_tensor_tensor(
                        xc, xp[:, j, k:k + 256], C("conv_w", 8 * k + tl_), xc, ALU.mult, ALU.add), t2)
            ir, br, fr = bank()
            ii, bi, fi = bank()
            for j in range(2):
                T(lambda e, j=j: e.matmul(br[:, 256 * j:256 * j + 256], rg[:, (2 * c + j) * 128:(2 * c + j + 1) * 128],
                                          Wt[0][:, 256 * j:256 * j + 256], start=True, stop=True), fr, t2, t_rg)
                t = T(lambda e, j=j: e.matmul(bi[:, 256 * j:256 * j + 256],
                                              rg[:, 1024 + (2 * c + j) * 128:1024 + (2 * c + j + 1) * 128],
                                              Wt[0][:, 256 * j:256 * j + 256], start=True, stop=True), fi, inc=True)
            if c == 3:
                done(s_rg, t)
            for j in range(2):
                tl_ = 2 * c + j
                sl = slice(256 * j, 256 * j + 256)
                t3 = A(lambda e, sl=sl, tl_=tl_: e.activation(Wt[1][:, sl], br[:, sl], ACT.Tanh, scale=0.5,
                                                              bias=hb[:, tl_:tl_ + 1]), t, t_hb, P.last("dve"))
                t4 = A(lambda e, sl=sl, tl_=tl_: e.activation(Wt[2][:, sl], bi[:, sl], ACT.Tanh, scale=0.5,
                                                              bias=hb[:, 8 + tl_:9 + tl_]))
            freed[ir], freed[ii] = t3, t4
            t3 = V(lambda e: e.tensor_scalar(Wt[1], Wt[1], 0.5, 0.5, ALU.mult, ALU.add), t3)
            t4 = V(lambda e: e.tensor_scalar(Wt[2], Wt[2], 0.5, 0.5, ALU.mult, ALU.add), t4)
            for j in range(2):
                tl_ = 2 * c + j
                sl = slice(256 * j, 256 * j + 256)
                t5 = A(lambda e, sl=sl, tl_=tl_: e.activation(Wt[3][:, sl], Wt[1][:, sl], ACT.Tanh,
                                                              scale=sp8[:, tl_:tl_ + 1]), t3, t_sp)
                t6 = A(lambda e, sl=sl, tl_=tl_: e.activation(Wt[4][:, sl], Wt[1][:, sl], ACT.Exp,
                                                              scale=sp8[:, 8 + tl_:9 + tl_]), t3)
            t7 = V(lambda e: e.tensor_scalar(Wt[5], Wt[3], 1.0, None, ALU.add), t5)
            t7 = V(lambda e: e.reciprocal(Wt[5], Wt[5]), t7)
            t7 = V(lambda e: e.scalar_tensor_tensor(Wt[3], Wt[3], 2.0, Wt[5], ALU.mult, ALU.mult), t7)
            t7 = A(lambda e: e.activation(Wt[3], Wt[3], ACT.Sqrt), t7)
            t8 = V(lambda e: e.tensor_tensor(Wt[2], Wt[2], Wt[0], ALU.mult), t4)
            t8 = V(lambda e: e.tensor_tensor(Wt[2], Wt[2], Wt[3], ALU.mult), t8, t7)
            for j in range(2):
                t9 = V(lambda e, j=j: e.tensor_tensor_scan(mix[:, 2 * c + j, :], Wt[4][:, 256 * j:256 * j + 256],
                                                           Wt[2][:, 256 * j:256 * j + 256], 0.0, ALU.mult, ALU.add),
                       t8, t6)
            t_mix[c] = t9
        for c in range(4):
            i, b, t = t_tile_chunk(4 + c)
            step(nstep)
            nstep += 1
            wt = Wt[c % 2]
            t1 = A(lambda e, wt=wt: e.activation(wt, b[:, :], ACT.Gelu_apprx_tanh), t, P.last("dve"))
            freed[i] = t1
            t_mix[c] = V(lambda e, wt=wt, c=c: e.tensor_tensor(mixv(c), mixv(c), wt, ALU.mult), t1, t_mix[c])
        for c in range(4):
            i, b, t = t_tile_chunk(20 + c)
            step(nstep)
            nstep += 1
            wt = Wt[2 + c % 2]
            t1 = A(lambda e, wt=wt: e.activation(wt, b[:, :], ACT.Sigmoid), t, P.last("dve"))
            freed[i] = t1
            t_mix[c] = V(lambda e, wt=wt, c=c: e.tensor_tensor(mixv(c), mixv(c), wt, ALU.mult), t1, t_mix[c])
        gate_b = []
        for c in range(4):
            i, b, t = t_tile_chunk(24 + c)
            step(nstep)
            nstep += 1
            wt = Wt[4 + c]
            t1 = A(lambda e, wt=wt: e.activation(wt, b[:, :], ACT.Sigmoid), t, P.last("dve"))
            freed[i] = t1
            gate_b.append((wt, t1))
        step(16)
        for c in range(4):
            wt, t1 = gate_b[c]
            yq = qk[0][:, 2 * c:2 * c + 2, :].rearrange("p a b -> p (a b)")
            t1 = V(lambda e, wt=wt, yq=yq: e.tensor_tensor(wt, wt, yq, ALU.mult), t1, att[2 * c], att[2 * c + 1])
            t_mix[c] = V(lambda e, wt=wt, c=c: e.tensor_tensor(mixv(c), mixv(c), wt, ALU.add), t1, t_mix[c])
        t_m1 = ada(a["ada_w"], 1, 0, "ada_b", t_c)
        t_m2 = ada(a["ada_w"], 2, 0, "ada_b", t_c)

        def project_add(w, src, t_src, blk, gate, scale=None):
            o = []
            for c in range(4):
                s, v, tl = load(w[c])
                i, b, fr = bank()
                t = tiles2(v, src, [tl, t_src], b=b, fr=fr)
                done(s, t)
                for j in range(2):
                    n = 2 * c + j
                    o.append(V(lambda e, j=j, n=n, b=b: e.scalar_tensor_tensor(
                        xT[:, n, :], b[:, 256 * j:256 * j + 256], modc[:, blk, gate + n:gate + n + 1], xT[:, n, :],
                        ALU.mult, ALU.add), t))
                freed[i] = o[-1]
            return o

        P.wait("dve", t_m1, t_m2)
        t_x1 = project_add(a["w_out"], mix, [t_mix[c] for c in range(4)], 0, 16)
        fence()

        sq = carve(8, 256)
        rst = carve(256)
        t_r = rms(xT[:, :, :], 8, D, sq, rst, 256)
        t_h = modulate(0, 3, "norm2", rst, sq, t_r)
        fence()

        ff = carve(24, 256)
        ub = [carve(2, 260) for _ in range(3)]
        cv = [carve(2, 256) for _ in range(3)]
        t_z = [V(lambda e, n=n: e.memset(ub[n][:, :, 0:2], 0.0)) for n in range(3)]
        t_cv = [None] * 3
        t_ff = None
        for j in range(24):
            s, v, tl = load(a["up"][j])
            i, b, fr = bank()
            t = tiles2(v, hT, [tl, t_h], b=b, fr=fr)
            done(s, t)
            u, w = ub[j % 3], cv[j % 3]
            t1 = A(lambda e, u=u, b=b: e.activation(u[:, :, 2:258], b[:, :].rearrange("p (a b) -> p a b", a=2),
                                                    ACT.Copy), t, t_z, t_cv[j % 3])
            freed[i] = t1
            ts = []
            for m in range(2):
                n = j + 24 * m
                t2 = V(lambda e, m=m, n=n, u=u, w=w: e.tensor_scalar(w[:, m, :], u[:, m, 2:258], C("fw", 96 + n),
                                                                     C("fb", n), ALU.mult, ALU.add), t1, t_cv[j % 3])
                for k in (1, 0):
                    t2 = V(lambda e, m=m, n=n, u=u, w=w, k=k: e.scalar_tensor_tensor(
                        w[:, m, :], u[:, m, k:k + 256], C("fw", 48 * k + n), w[:, m, :], ALU.mult, ALU.add), t2)
                ts.append(t2)
            t3 = A(lambda e, w=w: e.activation(w[:, 0, :], w[:, 0, :], ACT.Gelu_apprx_tanh), ts[0])
            t_ff = V(lambda e, j=j, w=w: e.tensor_tensor(ff[:, j, :], w[:, 0, :], w[:, 1, :], ALU.mult), t3, ts[1])
            t_cv[j % 3] = t_ff
        sl2 = sb("sl2", [128, 8])
        t = A(lambda e: e.activation(sl2[:, :], C("c2", 0, 8), ACT.Sigmoid), t_col)
        t = V(lambda e: e.tensor_tensor(sl2[:, :], sl2[:, :], C("c2", 0, 8), ALU.mult), t)
        t_c = make_crep(sl2, t)
        for g in range(3):
            t_m2 = ada(a["w_ada_2"], g, 1, "b_ada2", t_c)

        o = []
        for c in range(4):
            i0, b0, f0 = bank()
            i1, b1_, f1 = bank()
            for kk in range(3):
                s, v, tl = load(a["down"][c, kk])
                for k in range(8):
                    for j, bb in ((0, b0), (1, b1_)):
                        t = T(lambda e, k=k, j=j, bb=bb, kk=kk, v=v: e.matmul(
                            bb[:, 0:256], v[:, k * 256 + j * 128:k * 256 + j * 128 + 128], ff[:, kk * 8 + k, :],
                            start=(kk == 0 and k == 0), stop=(kk == 2 and k == 7)), f0, f1, tl, t_ff,
                            inc=(k == 7 and j == 1))
                done(s, t)
            for j, bb in ((0, b0), (1, b1_)):
                n = 2 * c + j
                t5 = V(lambda e, n=n, bb=bb: e.scalar_tensor_tensor(xT[:, n, :], bb[:, 0:256],
                                                                    modc[:, 0, 40 + n:41 + n], xT[:, n, :],
                                                                    ALU.mult, ALU.add), t)
                freed[(i0, i1)[j]] = t5
        fence()

        sq = carve(8, 256)
        rst = carve(256)
        t_r = rms(xT[:, :, :], 8, D, sq, rst, 256)
        t_h = modulate(1, 0, "pre_mix", rst, sq, t_r, t_m2)
        fence()

        cq, ckv = carve(2, 256), carve(256)
        qh, kh = carve(8, 256), carve(8, 256)
        vm, vd = carve(2, 512), carve(2, 128)
        qd, kd = carve(4, 256), carve(256)
        qi, ki = carve(2, 256), carve(256)
        widx = carve(2, 8)
        cs = carve(256)
        dist, isc, selb = carve(384), carve(384), carve(384)
        W = [carve(512) for _ in range(6)]
        st = carve(96)
        m8 = carve(8)

        s_p = [sem(f"p{n}") for n in range(8)]
        posr = W[5][:, 0:256].bitcast(I32)
        posc = carve(2).bitcast(I32)
        pi = W[4].bitcast(I32).rearrange("p (a b) -> p a b", a=2)
        pci = carve(2, 2).bitcast(I32)
        pcf = carve(2, 2)
        P.dma("sp", lambda e: e.dma_start(posr, a["posr"]), s_p[0], P.last("dve"), P.last("act"),
              P.last("pe"))
        P.dma("sp", lambda e: e.dma_start(posc, a["posc"]), s_p[1])
        serial[0] = True
        phi, plo = W[0][:, 0:256], W[0][:, 256:512]
        t = V(lambda e: e.tensor_single_scalar(pi[:, 0, :], posr, 12, ALU.arith_shift_right), (s_p[0], 16))
        t = V(lambda e: e.tensor_single_scalar(pi[:, 1, :], posr, 4095, ALU.bitwise_and), t)
        t1 = V(lambda e: e.tensor_single_scalar(pci[:, 0, :], posc, 12, ALU.arith_shift_right), (s_p[1], 16))
        t1 = V(lambda e: e.tensor_single_scalar(pci[:, 1, :], posc, 4095, ALU.bitwise_and), t1)
        t = V(lambda e: e.tensor_copy(phi, pi[:, 0, :]), t)
        t = V(lambda e: e.tensor_copy(plo, pi[:, 1, :]), t)
        t1 = V(lambda e: e.tensor_copy(pcf[:, :, :], pci[:, :, :]), t1)
        for tt, o0, w in ((0, 0, 128), (1, 128, 256)):
            d = dist[:, o0:o0 + w]
            t2 = V(lambda e: e.tensor_scalar(d, phi[:, 0:w], pcf[:, 0, tt:tt + 1], 4096.0, ALU.subtract, ALU.mult),
                   t, t1)
            t3 = V(lambda e: e.tensor_scalar(W[1][:, 0:w], plo[:, 0:w], pcf[:, 1, tt:tt + 1], None, ALU.subtract),
                   t, t1)
            t2 = V(lambda e: e.tensor_tensor(d, d, W[1][:, 0:w], ALU.add), t2, t3)
            t_dist = A(lambda e: e.activation(d, d, ACT.Abs), t2)
            P.wait("dve", t_dist)
        ang, r1, r2 = W[2][:, 0:256], W[2][:, 256:512], W[3][:, 0:256]
        r3 = W[3][:, 256:512]
        TP = two_pi_parts()
        t = V(lambda e: e.scalar_tensor_tensor(ang, phi, 4096.0, plo, ALU.mult, ALU.add), t)
        t = V(lambda e: e.tensor_scalar(ang, ang, K("freq"), None, ALU.mult), t, t_con)
        for _ in range(2):
            t = V(lambda e: e.tensor_scalar(r1, ang, 1.0 / (2.0 * np.pi), None, ALU.mult), t)
            t = V(lambda e: e.tensor_copy(pi[:, 0, :], r1), t)
            t = V(lambda e: e.tensor_copy(r1, pi[:, 0, :]), t)
            t = V(lambda e: e.tensor_single_scalar(r2.bitcast(I32), r1.bitcast(I32), -4096, ALU.bitwise_and), t)
            t = V(lambda e: e.tensor_tensor(r3, r1, r2, ALU.subtract), t)
            for part in TP:
                for r in (r2, r3):
                    t = V(lambda e: e.scalar_tensor_tensor(ang, r, -part, ang, ALU.mult, ALU.add), t)
        for sgn, cmp_ in ((-1.0, ALU.is_gt), (1.0, ALU.is_lt)):
            t = V(lambda e: e.tensor_scalar(r1, ang, -sgn * np.pi, sgn * 2.0 * np.pi, cmp_, ALU.mult), t)
            t = V(lambda e: e.tensor_tensor(ang, ang, r1, ALU.add), t)
        pi32 = float(np.nextafter(np.float32(np.pi), np.float32(0)))
        t = V(lambda e: e.tensor_scalar(ang, ang, pi32, -pi32, ALU.min, ALU.max), t)
        halfpi = sb("halfpi", [128, 1])
        t1 = V(lambda e: e.memset(halfpi[:, :], np.pi / 2))
        t2 = A(lambda e: e.activation(r1[64:96, :], ang[64:96, :], ACT.Abs), t)
        t2 = A(lambda e: e.activation(cs[64:96, :], r1[64:96, :], ACT.Sin, scale=-1.0, bias=halfpi[64:96, 0:1]),
               t2, t1)
        t3 = A(lambda e: e.activation(cs[96:128, :], ang[96:128, :], ACT.Sin), t)
        t_cs = V(lambda e: e.tensor_scalar(cs[96:128, :], cs[96:128, :], K("sign")[96:128, :], None, ALU.mult), t3)
        t_cs = [t_cs, t2]

        def chunk2(n):
            s, v, tl = load(a["w2in"][n])
            i, b, fr = bank()
            t = tiles2(v, hT, [tl, t_h], b=b, fr=fr)
            done(s, t)
            return i, b, t

        i, b, t = chunk2(4)
        t_qi = A(lambda e: e.activation(qi.rearrange("p a b -> p (a b)"), b[:, :], ACT.Copy), t)
        freed[i] = t_qi
        i, b, t = chunk2(5)
        t1 = A(lambda e: e.activation(ki, b[:, 0:256], ACT.Copy), t)
        t_ki = A(lambda e: e.activation(kd, b[:, 256:512], ACT.Copy), t)
        freed[i] = t_ki
        s, v, tl = load(a["wv"], 8 * 136)
        i, b, fr = bank()
        for tt in range(2):
            for k in range(8):
                t = T(lambda e: e.matmul(b[:, 256 * tt:256 * tt + 136], hT[:, k, tt * 128:(tt + 1) * 128],
                                         v[:, k * 136:(k + 1) * 136], start=(k == 0), stop=(k == 7)),
                      fr, tl, t_h, inc=(tt == 1 and k == 7))
        done(s, t)
        bv = b[:, :].rearrange("p (a b) -> p a b", a=2)
        t_vd = A(lambda e: e.activation(vd, bv[:, :, 0:128], ACT.Copy), t)
        t_w = A(lambda e: e.activation(widx, bv[:, :, 128:136], ACT.Copy, scale=float(8 ** -0.5 * 32 ** -0.5)), t)
        freed[i] = t_w
        t_is = None
        for h in range(8):
            r, tq = 32 * (h % 4), h // 4
            i, b, fr = bank()
            T(lambda e: e.matmul(b[:, 0:128], qi[r:r + 32, tq, 0:128], ki[r:r + 32, 0:128], start=True, stop=True),
              fr, t_qi, t_ki)
            t = T(lambda e: e.matmul(b[:, 128:384], qi[r:r + 32, tq, 128:256], ki[r:r + 32, 0:256], start=True,
                                     stop=True), inc=True)
            dst = isc if h == 0 else W[4][:, 0:384]
            V(lambda e: e.tensor_scalar(dst[:, 0:128], b[:, 0:128], 0.0, widx[:, 0, h:h + 1], ALU.max, ALU.mult),
              t, t_w, t_is)
            t = V(lambda e: e.tensor_scalar(dst[:, 128:384], b[:, 128:384], 0.0, widx[:, 1, h:h + 1], ALU.max,
                                            ALU.mult))
            freed[i] = t
            if h:
                t_is = V(lambda e: e.tensor_tensor(isc, isc, dst, ALU.add), t, t_is)
            else:
                t_is = t
        t_is = V(lambda e: e.tensor_tensor(isc, isc, K("cbias"), ALU.add), t_is)

        def topk():
            for lo, hi in ((0, 128), (128, 384)):
                sv = isc[:, lo:hi]
                t = t_is
                for _ in range(8):
                    t = V(lambda e: e.max(m8, sv), t)
                    t = V(lambda e: e.match_replace(sv, m8, sv, -3e38), t)
            t = V(lambda e: e.tensor_scalar(selb, isc, -2e38, NEG, ALU.is_gt, ALU.mult), t)
            return V(lambda e: e.tensor_tensor(selb, selb, K("cbias"), ALU.add), t)

        t_sel = topk()

        i, b, t = chunk2(0)
        cqf = cq.rearrange("p a b -> p (a b)")
        t1 = V(lambda e: e.tensor_copy(cqf, b[:, :]), t)
        freed[i] = t1
        t2 = rms(cq, 2, 256, W[0].rearrange("p (a b) -> p a b", a=2), W[1][:, 0:256], 256, t1)
        for k in range(2):
            t_cq = V(lambda e: e.scalar_tensor_tensor(cq[:, k, :], cq[:, k, :], C("gq", k), W[1][:, 0:256], ALU.mult,
                                                      ALU.mult), t2)
        i, b, t = chunk2(1)
        t1 = V(lambda e: e.tensor_copy(ckv, b[:, 0:256]), t)
        t2 = V(lambda e: e.tensor_tensor(W[5][64:96, 0:256], b[64:96, 256:512], cs[64:96, :], ALU.mult), t, t_cs)
        t3 = V(lambda e: e.tensor_tensor(W[5][64:96, 256:512], b[96:128, 256:512], cs[96:128, :], ALU.mult), t)
        freed[i] = t3
        t3 = V(lambda e: e.tensor_tensor(W[5][64:96, 0:256], W[5][64:96, 0:256], W[5][64:96, 256:512], ALU.add),
               t2, t3)
        t_kr = V(lambda e: e.tensor_copy(kh[64:96, :, :],
                                         W[5][64:96, 0:256].unsqueeze(1).to_broadcast([32, 8, 256])), t3)
        t2 = rms(ckv, 1, 128, W[0][:, 0:256], W[1][:, 0:256], 256, t1, t_cq)
        t_ckv = V(lambda e: e.scalar_tensor_tensor(ckv, ckv, C("gkv"), W[1][:, 0:256], ALU.mult, ALU.mult), t2)
        for n in (2, 3):
            i, b, t = chunk2(n)
            t_qd = A(lambda e: e.activation(qd[:, 2 * n - 4:2 * n - 2, :].rearrange("p a b -> p (a b)"), b[:, :],
                                            ACT.Copy, scale=0.125), t)
            freed[i] = t_qd
        s, v, tl = load(a["qb"])
        t_qh = []
        for p in range(4):
            i, b, fr = bank()
            for j in range(2):
                for k in range(2):
                    h = 2 * p + j
                    t = T(lambda e: e.matmul(b[:, 256 * j:256 * j + 256],
                                             v[:, k * 1024 + h * 128:k * 1024 + h * 128 + 128], cq[:, k, :],
                                             start=(k == 0), stop=(k == 1)), fr, tl, t_cq, inc=(j == 1 and k == 1))
            bv = b[:, :].rearrange("p (a b) -> p a b", a=2)
            wv_ = W[4].rearrange("p (a b) -> p a b", a=2)
            t1 = A(lambda e: e.activation(qh[0:64, 2 * p:2 * p + 2, :], bv[0:64], ACT.Copy), t)
            t2 = V(lambda e: e.tensor_tensor(qh[64:96, 2 * p:2 * p + 2, :], bv[64:96],
                                             cs[64:96, :].unsqueeze(1).to_broadcast([32, 2, 256]), ALU.mult), t, t_cs)
            t3 = V(lambda e: e.tensor_tensor(wv_[64:96], bv[96:128],
                                             cs[96:128, :].unsqueeze(1).to_broadcast([32, 2, 256]), ALU.mult), t)
            freed[i] = [t1, t3]
            t3 = V(lambda e: e.tensor_tensor(qh[64:96, 2 * p:2 * p + 2, :], qh[64:96, 2 * p:2 * p + 2, :], wv_[64:96],
                                             ALU.add), t2, t3)
            t_qh += [t1, t3]
        done(s, t)
        s, v, tl = load(a["kvb"], 1024)
        for p in range(4):
            i, b, fr = bank()
            for j in range(2):
                h = 2 * p + j
                t = T(lambda e: e.matmul(b[0:64, 256 * j:256 * j + 256], v[:, h * 64:h * 64 + 64], ckv, start=True,
                                         stop=True), fr, tl, t_ckv, inc=(j == 1))
            t_kh = A(lambda e: e.activation(kh[0:64, 2 * p:2 * p + 2, :].rearrange("p a b -> p (a b)"), b[0:64, :],
                                            ACT.Copy), t)
            freed[i] = t_kh
        for tt in range(2):
            i, b, fr = bank()
            t = T(lambda e: e.matmul(b[:, :], ckv[:, tt * 128:(tt + 1) * 128], v[:, 512:1024], start=True, stop=True),
                  fr, inc=True)
            t_vm = A(lambda e: e.activation(vm[:, tt, :], b[:, :], ACT.Copy), t)
            freed[i] = t_vm
        done(s, t)
        fence_tokens = [P.last("dve"), P.last("act"), P.last("pe")]

        mix2 = hT
        heads = {}
        ybank = {}
        wfree = [None] * 3
        pfree = [None] * 3

        def head_scores(n):
            i, b, fr = bank()
            if n < 8:
                ks, qs = kh[0:96, n, :], qh[0:96, n, :]
                dep = [t_qh, t_kh, t_kr]
            else:
                h = n - 8
                r = 64 * (h // 4)
                ks, qs = kd[r:r + 64, :], qd[r:r + 64, h % 4, :]
                dep = [t_qd, t_ki]
            T(lambda e: e.matmul(b[:, 0:128], qs[:, 0:128], ks[:, 0:128], start=True, stop=True), fr, dep)
            t = T(lambda e: e.matmul(b[:, 128:384], qs[:, 128:256], ks[:, 0:256], start=True, stop=True), inc=True)
            w = W[n % 3][:, 0:384]
            so = st[:, 6 * n:6 * n + 6]
            if n < 8:
                t = V(lambda e: e.scalar_tensor_tensor(w, b[:, 0:384], float(96 ** -0.5), K("cbias"), ALU.mult,
                                                       ALU.add), t, wfree[n % 3], fence_tokens)
                freed[i] = t
            else:
                slope = float(2.0 ** -(n - 8 + 1))
                t = V(lambda e: e.scalar_tensor_tensor(w, dist, -slope, b[:, 0:384], ALU.mult, ALU.add), t,
                      wfree[n % 3], fence_tokens, t_dist)
                freed[i] = t
                t = V(lambda e: e.tensor_tensor(w, w, selb, ALU.add), t, t_sel)
            seg = ((0, 0, 128), (1, 128, 384))
            for tt, lo, hi in seg:
                t1 = V(lambda e: e.tensor_reduce(so[:, tt:tt + 1], w[:, lo:hi], AX.X, ALU.max, negate=True), t)
            for tt, lo, hi in seg:
                t2 = A(lambda e: e.activation(w[:, lo:hi], w[:, lo:hi], ACT.Exp, bias=so[:, tt:tt + 1],
                                              accum_out=so[:, 2 + tt:3 + tt]), t1)
            t3 = V(lambda e: e.reciprocal(so[:, 4:6], so[:, 2:4]), t2)
            for tt, lo, hi in seg:
                t3_ = V(lambda e: e.tensor_scalar(w[:, lo:hi], w[:, lo:hi], so[:, 4 + tt:5 + tt], None, ALU.mult), t3)
            heads[n] = t3_

        def head_out(n):
            w = W[n % 3][:, 0:384]
            pt = W[3 + n % 3][:, 0:384]
            i, b, fr = bank()
            for q in range(3):
                t = T(lambda e: e.transpose(b[:, 128 * q:128 * q + 128], w[:, 128 * q:128 * q + 128], K("ident")),
                      fr, heads[n], inc=(q == 2))
            wfree[n % 3] = t
            t = A(lambda e: e.activation(pt, b[:, 0:384], ACT.Copy), t, pfree[n % 3], fence_tokens)
            freed[i] = t
            if n % 2 == 0:
                ybank[n // 2] = bank()
            iy, by, fr = ybank[n // 2]
            r = 64 * (n % 2)
            if n < 8:
                v0, v1 = vm[:, 0, n * 64:n * 64 + 64], vm[:, 1, n * 64:n * 64 + 64]
            else:
                o0 = 64 * ((n - 8) // 4)
                v0, v1 = vd[:, 0, o0:o0 + 64], vd[:, 1, o0:o0 + 64]
            T(lambda e: e.matmul(by[r:r + 64, 0:256], v0, pt[:, 0:256], start=True, stop=False,
                                 skip_group_check=True), fr, t, t_vm, t_vd)
            t = T(lambda e: e.matmul(by[r:r + 64, 128:256], v1, pt[:, 256:384], start=False, stop=True,
                                     skip_group_check=True), inc=True)
            pfree[n % 3] = t
            if n % 2:
                t1 = V(lambda e: e.tensor_copy(mix2[:, n // 2, :], by[:, 0:256]), t)
                freed[iy] = t1
                heads[n] = t1

        for n in range(18):
            if n < 16:
                head_scores(n)
            if n >= 2:
                head_out(n - 2)
        t_mx = [heads[n] for n in range(1, 16, 2)]

        mo = qh
        sq = kh
        for c in range(4):
            s, v, tl = load(a["w_o"][c])
            i, b, fr = bank()
            t = tiles2(v, mix2, [tl, t_mx], b=b, fr=fr)
            done(s, t)
            t_mo = V(lambda e: e.tensor_copy(mo[:, 2 * c:2 * c + 2, :].rearrange("p a b -> p (a b)"), b[:, :]), t)
            freed[i] = t_mo
        t_r = rms(mo, 8, D, sq, W[0][:, 0:256], 256, t_mo, P.last("pe"))
        t1 = V(lambda e: e.tensor_tensor(mc[:, 8:16], modc[:, 1, 16:24], C("post_mix", 0, 8), ALU.mult))
        t2 = V(lambda e: e.tensor_tensor(mo, mo, W[0][:, 0:256].unsqueeze(1).to_broadcast([128, 8, 256]), ALU.mult),
               t_r)
        for k in range(8):
            t_x = V(lambda e: e.scalar_tensor_tensor(xT[:, k, :], mo[:, k, :], mc[:, 8 + k:9 + k], xT[:, k, :],
                                                     ALU.mult, ALU.add), t1, t2)
        fence()
        sq = carve(8, 256)
        rst = carve(256)
        t_r = rms(xT[:, :, :], 8, D, sq, rst, 256)
        t_h = modulate(1, 3, "pre_ffn", rst, sq, t_r)
        fence()

        h4 = carve(2, 1024)
        acc = carve(2, 1024)
        lg, mk, gt, posm = carve(2, 32), carve(2, 32), carve(2, 32), carve(2, 32)
        tmp = [carve(2, 32) for _ in range(3)]
        sm = carve(32)
        mm8 = carve(2, 8)
        zer = carve(32)
        cntf = carve(32)
        gT = carve(2, 128)
        xe = [[carve(512), carve(512)] for _ in range(2)]
        selT = [[carve(256), carve(256)] for _ in range(2)]
        xg = carve(512)
        sel = [carve(2, 64) for _ in range(2)]
        selg = [carve(2, 128) for _ in range(2)]
        w0, w1, w2 = [carve(512) for _ in range(3)]
        actb = [w0, carve(512)]
        b1h = carve(1024)[0:96].bitcast(BF16)
        sel96 = carve(1024)[0:96].bitcast(BF16)
        cnti = sb("cnti", [128, 33], I32)

        s_wr, v, tl = load(a["wr"], 256)
        i, b, fr = bank()
        for tt in range(2):
            for k in range(8):
                t = T(lambda e: e.matmul(b[:, 32 * tt:32 * tt + 32], hT[:, k, tt * 128:(tt + 1) * 128],
                                         v[:, k * 32:(k + 1) * 32], start=(k == 0), stop=(k == 7)),
                      fr, tl, inc=(tt == 1 and k == 7))
        done(s_wr, t)
        brt = sb("brt", [128, 32])
        P.dma("sp", lambda e: e.dma_start(brt[:, :], a["br"]), s_p[2])
        t_lg = V(lambda e: e.tensor_tensor(lg, b[:, 0:64].rearrange("p (a b) -> p a b", a=2),
                                           brt[:, :].unsqueeze(1).to_broadcast([128, 2, 32]), ALU.add),
                 t, (s_p[2], 16))
        freed[i] = t_lg
        t_z = V(lambda e: e.memset(zer, 0.0))
        t_g = []
        for tt in range(2):
            l = lg[:, tt, :]
            gtt, cum, eq = tmp[0][:, tt, :], tmp[1][:, tt, :], tmp[2][:, tt, :]
            so = sm[:, 8 * tt:8 * tt + 8]
            t = V(lambda e: e.max(mm8[:, tt, :], l), t_lg)
            v4 = mm8[:, tt, 3:4]
            t1 = V(lambda e: e.tensor_scalar(gtt, l, v4, 0.0, ALU.is_gt, ALU.add, accum_out=so[:, 0:1]), t)
            t2 = V(lambda e: e.tensor_scalar(eq, l, v4, None, ALU.is_equal), t)
            t2 = V(lambda e: e.tensor_tensor_scan(cum, eq, zer, 0.0, ALU.add, ALU.add), t2, t_z)
            t1 = V(lambda e: e.tensor_scalar(so[:, 1:2], so[:, 0:1], -1.0, 4.0, ALU.mult, ALU.add), t1)
            t2 = V(lambda e: e.scalar_tensor_tensor(eq, cum, so[:, 1:2], eq, ALU.is_le, ALU.mult), t1, t2)
            t_mk = V(lambda e: e.tensor_tensor(mk[:, tt, :], gtt, eq, ALU.add), t2)
            t3 = V(lambda e: e.tensor_scalar(so[:, 2:3], mm8[:, tt, 0:1], -1.0, None, ALU.mult), t)
            t3 = A(lambda e: e.activation(cum, l, ACT.Exp, bias=so[:, 2:3]), t3, t2)
            t3 = V(lambda e: e.tensor_tensor(cum, cum, mk[:, tt, :], ALU.mult), t3, t_mk)
            t3 = V(lambda e: e.tensor_reduce(so[:, 3:4], cum, AX.X, ALU.add), t3)
            t3 = V(lambda e: e.reciprocal(so[:, 4:5], so[:, 3:4]), t3)
            t_g.append(V(lambda e: e.tensor_scalar(gt[:, tt, :], cum, so[:, 4:5], None, ALU.mult), t3))
        i, b, fr = bank()
        T(lambda e: e.matmul(b[:, 0:32], K("uinc"), mk[:, 0, :], start=True, stop=True), fr, t_mk)
        T(lambda e: e.matmul(b[:, 32:64], K("ones"), mk[:, 0, :], start=True, stop=False))
        T(lambda e: e.matmul(b[:, 32:64], K("uinc"), mk[:, 1, :], start=False, stop=True))
        T(lambda e: e.matmul(b[:, 64:96], K("ones"), mk[:, 0, :], start=True, stop=False))
        t = T(lambda e: e.matmul(b[:, 64:96], K("ones"), mk[:, 1, :], start=False, stop=True), inc=True)
        t1 = V(lambda e: e.tensor_tensor(posm, b[:, 0:64].rearrange("p (a b) -> p a b", a=2), mk, ALU.mult), t)
        t2 = V(lambda e: e.tensor_copy(cntf, b[:, 64:96]), t)
        freed[i] = t2
        t_pos = V(lambda e: e.tensor_scalar(posm, posm, -1.0, None, ALU.add), t1)
        t_ci = V(lambda e: e.tensor_copy(cnti[:, 0:32], cntf), t2)
        t_ci = V(lambda e: e.tensor_reduce(cnti[:, 32:33], cntf, AX.X, ALU.max), t2)
        for tt in range(2):
            for q in range(2):
                i, b, fr = bank()
                for k in range(4):
                    t = T(lambda e: e.transpose(b[:, 128 * k:128 * k + 128],
                                                hT[:, 4 * q + k, tt * 128:(tt + 1) * 128], K("ident")), fr,
                          inc=(k == 3))
                t_h4 = A(lambda e: e.activation(h4[:, tt, q * 512:(q + 1) * 512], b[:, :], ACT.Copy), t)
                freed[i] = t_h4
        s_b2, vb2, tl = load(a["b2"], 1024)
        i, b, fr = bank()
        for tt in range(2):
            t = T(lambda e: e.transpose(b[0:32, 128 * tt:128 * tt + 128], gt[:, tt, :], K("ident")), fr, t_g,
                  inc=True)
        t = V(lambda e: e.tensor_copy(gT[0:32].rearrange("p a b -> p (a b)"), b[0:32, 0:256]), t)
        freed[i] = t
        t_acc = []
        for tt in range(2):
            for q in range(2):
                i, b, fr = bank()
                t1 = T(lambda e: e.matmul(b[:, :], gT[0:32, tt, :], vb2[0:32, q * 512:(q + 1) * 512], start=True,
                                          stop=True), fr, tl, t, inc=True)
                t_acc.append(V(lambda e: e.tensor_copy(acc[:, tt, q * 512:(q + 1) * 512], b[:, :]), t1))
                freed[i] = t_acc[-1]
        done(s_b2, t1)
        s_b1, vb1, tl = load(a["b1"], 2048)
        t = tl
        for q in range(4):
            src = vb1[0:96, q * 512:(q + 1) * 512]
            fb, ff_ = w0[0:96, :], w1[0:96, :]
            hb16 = w2[0:96, 0:256].bitcast(BF16)
            dst = b1h[:, q * 512:(q + 1) * 512]
            t = V(lambda e: e.tensor_copy(hb16, src), t)
            t = V(lambda e: e.tensor_copy(dst[0:32], hb16[0:32]), t)
            t = V(lambda e: e.tensor_copy(fb, hb16), t)
            t = V(lambda e: e.tensor_tensor(ff_, src, fb, ALU.subtract), t)
            t = V(lambda e: e.tensor_copy(hb16, ff_), t)
            t = V(lambda e: e.tensor_copy(dst[32:64], hb16[32:64]), t)
            t = V(lambda e: e.tensor_copy(fb, hb16), t)
            t = V(lambda e: e.tensor_tensor(ff_, ff_, fb, ALU.subtract), t)
            t = V(lambda e: e.tensor_copy(dst[64:96], ff_[64:96]), t)
        t_b1 = t
        done(s_b1, t)
        s_s, vs, tl = load(a["sel96"])
        t_s96 = V(lambda e: e.tensor_copy(sel96, vs[0:96, :]), tl)
        done(s_s, t_s96)
        fence_tokens = [P.last(e) for e in ("pe", "act", "dve")]
        for e_ in ("pe", "act", "dve"):
            P.wait(e_, fence_tokens, [freed[n] for n in range(8)])

        P.wait("sp", t_ci)
        for e_ in ("pe", "act", "dve"):
            P.wait(e_, t_ci, t_b1, t_s96, t_pos, t_g)
        serial[0] = False
        HID = [[B[0], B[1]], [B[2], B[3]]]
        OUT = [[B[4], B[5]], [B[6], B[7]]]
        spare = hT[:, :, :].rearrange("p a b -> p (a b)")
        aT = [spare[:, 0:512], spare[:, 512:1024]]
        ysb = [spare[:, 1024:1536], spare[:, 1536:2048]]
        tok = {}

        def gather(x, c):
            io = K("iota", 128 * c, 128 * c + 128)
            xb, sb_ = xe[c][x % 2], selT[c][x % 2]
            for tt in range(2):
                t_s = V(lambda e: e.tensor_scalar(sel[c][:, tt, :], io[:, 0:64], posm[:, tt, x:x + 1], None,
                                                  ALU.is_equal), tok.get(("sel", c)))
            for tt in range(2):
                t_sg = V(lambda e: e.tensor_scalar(selg[c][:, tt, :], io, posm[:, tt, x:x + 1],
                                                   gt[:, tt, x:x + 1], ALU.is_equal, ALU.mult), tok.get(("selg", c)))
            for tt in range(2):
                for hf in range(2):
                    t = T(lambda e: e.matmul(B[3][64 * hf:64 * hf + 64, :], sel[c][:, tt, :],
                                             h4[:, tt, hf * 512:(hf + 1) * 512], start=(tt == 0), stop=(tt == 1),
                                             skip_group_check=True), t_s, freed[3], inc=(tt == 1 and hf == 1))
            tok["sel", c] = t
            t_xg = A(lambda e: e.activation(xg, B[3][:, :], ACT.Copy), t, tok.get("xg"))
            for tt in range(2):
                t = T(lambda e: e.transpose(B[2][:, 128 * tt:128 * tt + 128], selg[c][:, tt, :], K("ident")), t_sg,
                      freed[2], inc=(tt == 1))
            tok["selg", c] = t
            t_sT = V(lambda e: e.tensor_copy(sb_, B[2][:, 0:256]), t, tok.get(("selT", c, x % 2)))
            freed[2] = t_sT
            for q in range(4):
                t = T(lambda e: e.transpose(B[3][:, 128 * q:128 * q + 128], xg[:, 128 * q:128 * q + 128],
                                            K("ident")), t_xg, inc=(q == 3))
            tok["xg"] = t
            t_xe = A(lambda e: e.activation(xb, B[3][:, :], ACT.Copy), t, tok.get(("xe", c, x % 2)))
            freed[3] = t_xe
            tok["gathered", c, x] = (t_xe, t_sT)

        def up(x, cs, pieces_):
            for c in cs:
                for n in range(2):
                    for hf in range(2):
                        o0 = hf * 1024 + n * 512
                        T(lambda e: e.matmul(HID[c][n][64 * hf:64 * hf + 64, :], sel96[:, x * 64:(x + 1) * 64],
                                             b1h[:, o0:o0 + 512], start=True, stop=False, skip_group_check=True),
                          [freed[0], freed[1]] if c == 0 else [freed[2], freed[3]])
            o = []
            for k in range(8):
                s, v, tl = pieces_[k]
                xo = 128 * (k % 4) + 64 * (k // 4)
                for c in cs:
                    for n in range(2):
                        for hf in range(2):
                            o0 = hf * 1024 + n * 512
                            t = T(lambda e: e.matmul(HID[c][n][64 * hf:64 * hf + 64, :],
                                                     xe[c][x % 2][:, xo:xo + 64], v[:, o0:o0 + 512], start=False,
                                                     stop=(k == 7), skip_group_check=True),
                                  tl, tok["gathered", c, x][0], inc=(c == cs[-1] and n == 1 and hf == 1))
                o.append(t)
            return o

        def act(c, t):
            ts = []
            for n in range(2):
                hv = HID[c][n][:, :].rearrange("p (f two) -> p f two", two=2)
                sl = slice(256 * n, 256 * n + 256)
                tg = V(lambda e: e.tensor_scalar(actb[c][:, sl], hv[:, :, 0], 7.0, None, ALU.min), t,
                       tok.get(("actb", c)), tok.get("w"))
                tl2 = V(lambda e: e.tensor_scalar(w1[:, sl], hv[:, :, 1], -7.0, 7.0, ALU.max, ALU.min), t)
                tsg = A(lambda e: e.activation(w2[:, sl], actb[c][:, sl], ACT.Sigmoid, scale=1.702), tg, tok.get("w"))
                t3 = V(lambda e: e.scalar_tensor_tensor(w1[:, sl], w1[:, sl], 1.0, actb[c][:, sl], ALU.add,
                                                        ALU.mult), tg, tl2)
                freed[2 * c + n] = tl2
                ts.append((sl, t3, tsg))
            o = [V(lambda e: e.tensor_tensor(actb[c][:, sl], w1[:, sl], w2[:, sl], ALU.mult), t3, tsg)
                 for sl, t3, tsg in ts]
            tok["w"] = o
            return o

        def turn_act(c, ts):
            for q in range(4):
                t = T(lambda e: e.transpose(B[2 + c][:, 128 * q:128 * q + 128], actb[c][:, 128 * q:128 * q + 128],
                                            K("ident")), freed[2 + c], ts[q // 2], inc=(q == 3))
            tok["actb", c] = t
            t = A(lambda e: e.activation(aT[c], B[2 + c][:, :], ACT.Copy), t, tok.get(("aT", c)))
            freed[2 + c] = t
            return t

        def down(x, cs, ta, pieces_, new):
            o = []
            for kt in range(8):
                s, v, tl = pieces_[kt // 2]
                q, hf = kt % 4, kt // 4
                for c in cs:
                    for oh in range(2):
                        t = T(lambda e: e.matmul(B[2 + c][64 * oh:64 * oh + 64, :],
                                                 aT[c][:, 128 * q + 64 * hf:128 * q + 64 * hf + 64],
                                                 v[:, (kt % 2) * 1024 + oh * 512:(kt % 2) * 1024 + oh * 512 + 512],
                                                 start=(kt == 0), stop=(kt == 7), skip_group_check=True), ta[c], tl,
                              inc=(kt % 2 == 1 and c == cs[-1] and oh == 1))
                if kt % 2:
                    o.append(t)
            for c in cs:
                tok["aT", c] = t
                ty = A(lambda e: e.activation(ysb[c], B[2 + c][:, :], ACT.Copy), o[-1], tok.get(("y", c)))
                freed[2 + c] = ty
                for tt in range(2):
                    for oh in range(2):
                        t = T(lambda e: e.matmul(OUT[tt][oh][:, :],
                                                 selT[c][x % 2][64 * oh:64 * oh + 64, tt * 128:(tt + 1) * 128],
                                                 ysb[c][64 * oh:64 * oh + 64, :], start=(new and c == 0), stop=False,
                                                 skip_group_check=True), ty, tok["gathered", c, x][1],
                              inc=(tt == 1 and oh == 1))
                tok["y", c] = t
                tok["selT", c, x % 2] = t
            return o

        w1_v = a["w_mlp1"].rearrange("x (k p) n -> x k p n", p=128)
        w2_v = a["w_mlp2"].rearrange("x (m k p) n -> x m p k n", p=128, k=2)
        plan = []
        for x in range(NE):
            plan += [(w1_v[x, k], 1) for k in range(8)] + [(w2_v[x, m], 2) for m in range(4)]
        phase_sems = [sem(f"wl{n}") for n in range(RING)]
        slot_sem[:] = phase_sems
        slot_use[:] = [0] * RING
        again = []
        ahead = []
        for src, _ in plan[:RING]:
            s = piece[0] % RING
            ahead.append(load(src))
            again.append((slot_view(s, src, SLOT), src, phase_sems[s]))
        P.new_semaphores("_l")
        engines = ("pe", "act", "dve", "sp")

        def rest(e):
            return e.value_load(cnti[0:1, 32:33], min_val=-1000, max_val=256)

        P.begin_loop(engines, rest)
        for n in range(8):
            freed[n] = None
        nload = [RING]

        def next_pieces(n):
            o = []
            while len(queue) < n:
                queue.append(load(plan[nload[0]][0]))
                nload[0] += 1
            for _ in range(n):
                o.append(queue.pop(0))
            return o

        queue = list(ahead)
        for s, _, _ in ahead:
            slot_free[s] = False
        many = {}

        def lists(x):
            gather(x, 0)
            n = {}
            for me_ in ("pe", "act", "dve"):
                if P.me == me_:
                    n[me_] = P.eng.value_load(cnti[0:1, x:x + 1], min_val=-1000, max_val=256) > CAP
            many[x] = n.get(P.me)
            P.begin_if(("pe", "act", "dve"), many[x])
            gather(x, 1)
            P.end_if()

        lists(0)
        for x in range(NE):
            if x + 1 < NE:
                lists(x + 1)
            p1 = next_pieces(8)
            P.begin_if(("pe",), many[x])
            tk = up(x, (0, 1), p1)
            P.begin_else()
            up(x, (0,), p1)
            P.end_if()
            for (s, _, _), t in zip(p1, tk):
                done(s, t)
            tok["xe", 0, x % 2] = tok["xe", 1, x % 2] = tk[-1]
            ta = {}
            ts = act(0, tk[-1])
            P.begin_if(("act", "dve", "pe"), many[x])
            t1_ = act(1, tk[-1])
            ta[1] = turn_act(1, t1_)
            P.end_if()
            freed[2] = [freed[2], P.last("dve")]
            ta[0] = turn_act(0, ts)
            p2 = next_pieces(4)
            kept = dict(freed), dict(tok)
            P.begin_if(("pe", "act"), many[x])
            td = down(x, (0, 1), ta, p2, x == 0)
            P.begin_else()
            freed.update(kept[0])
            tok.clear()
            tok.update(kept[1])
            down(x, (0,), ta, p2, x == 0)
            P.end_if()
            for (s, _, _), t in zip(p2, td):
                done(s, t)
            for n in (2, 3):
                freed[n] = P.last("act")
            for c in (0, 1):
                tok["y", c] = tok["selT", c, x % 2] = tok["aT", c] = P.last("pe")
        serial[0] = True
        for tt in range(2):
            for q in range(2):
                V(lambda e: e.tensor_tensor(acc[:, tt, q * 512:(q + 1) * 512], OUT[tt][q][:, :],
                                            acc[:, tt, q * 512:(q + 1) * 512], ALU.add), P.last("pe"))
        P.wait("dve", P.last("act"), P.last("pe"))
        V(lambda e: e.tensor_scalar(posm, posm, -2.0 * CAP, None, ALU.add))
        V(lambda e: e.tensor_scalar(cntf, cntf, -2.0 * CAP, None, ALU.add))
        V(lambda e: e.tensor_copy(cnti[:, 0:32], cntf))
        V(lambda e: e.tensor_reduce(cnti[:, 32:33], cntf, AX.X, ALU.max))
        clear = [P.sem[e] for e in ("pe", "act", "dve")] + phase_sems
        go = {e: sem("go_" + e) for e in ("pe", "act", "dve")}
        P.end_loop(rest, clear, sem("bar"), go, again)

        ss = sm
        t_f = []
        for tt in range(2):
            t = A(lambda e: e.activation(h4[:, tt, :], acc[:, tt, :], ACT.Square, accum_out=ss[:, tt:tt + 1]))
            t = A(lambda e: e.activation(ss[:, 2 + tt:3 + tt], ss[:, tt:tt + 1], ACT.Sqrt, bias=eps[:, 0:1],
                                         scale=1.0 / D), t)
            t = V(lambda e: e.reciprocal(ss[:, 4 + tt:5 + tt], ss[:, 2 + tt:3 + tt]), t)
            t_f.append(V(lambda e: e.tensor_scalar(acc[:, tt, :], acc[:, tt, :], ss[:, 4 + tt:5 + tt], None,
                                                   ALU.mult), t))
        pool_banks[0] = list(range(8))
        for n in (4, 5, 6, 7):
            freed[n] = t_f
        for n in (0, 1, 2, 3):
            freed[n] = None
        t_c1 = V(lambda e: e.tensor_tensor(mc[:, 0:8], modc[:, 1, 40:48], C("post_ffn", 0, 8), ALU.mult))
        s_out = sem("s_out")
        for c in range(4):
            i, b, fr = bank()
            for j in range(2):
                for tt in range(2):
                    t = T(lambda e: e.transpose(b[:, 256 * j + 128 * tt:256 * j + 128 * tt + 128],
                                                acc[:, tt, (2 * c + j) * 128:(2 * c + j + 1) * 128], K("ident")), fr,
                          t_f, inc=(j == 1 and tt == 1))
            for j in range(2):
                n = 2 * c + j
                t_x = V(lambda e: e.scalar_tensor_tensor(xT[:, n, :], b[:, 256 * j:256 * j + 256], mc[:, n:n + 1],
                                                         xT[:, n, :], ALU.mult, ALU.add), t, t_c1)
            P.dma("sp", lambda e: e.dma_start(out[:, 2 * c:2 * c + 2, :], xT[:, 2 * c:2 * c + 2, :]), s_out, t_x)
        P.wait("sp", (s_out, 64))



def lay_out(i):
    def np_(n):
        return np.asarray(i[n])

    def cols(n):
        return np_(n).reshape(-1, 128).T

    def pieces(w, width=256):
        k, n = w.shape
        return np.ascontiguousarray(w.reshape(k // 128, 128, n // width, width).transpose(2, 1, 0, 3)).reshape(
            n // width, 128, k // 128 * width)

    o = {}
    o["xT"] = np.ascontiguousarray(np_("x")[0].T.reshape(8, 128, 256).transpose(1, 0, 2))
    order = ["c", "c_2", "ada_b", "b_ada_2", "norm1_g", "norm2_g", "conv_w", "conv_b", "rg_ba", "rg_bx", "rg_lambda",
             "q_norm_g", "k_norm_g", "ffn_conv_w", "ffn_conv_b", "g_pre_mix_2", "g_post_mix_2", "g_pre_ffn_2",
             "g_post_ffn_2", "g_q_a_2", "g_kv_a_2"]
    o["cols"] = np.ascontiguousarray(np.concatenate([cols(n) for n in order], 1))
    o["consts"] = constants()
    o["ada_w"] = np_("ada_w")[0]
    o["w_ada_2"] = np_("w_ada_2")[0]
    o["w_in"] = pieces(np_("w_in")[0])
    o["rg"] = np.ascontiguousarray(np.concatenate([np_("rg_wa")[0], np_("rg_wx")[0]], 0).transpose(1, 0, 2)).reshape(
        128, 2048)
    o["w_out"] = pieces(np_("w_out")[0])
    up = np_("ffn_up")[0].reshape(8, 128, 2, 24, 128)
    o["up"] = np.ascontiguousarray(up.transpose(3, 1, 0, 2, 4)).reshape(24, 128, 2048)
    dn = np_("ffn_down")[0].reshape(3, 8, 128, 4, 256)
    o["down"] = np.ascontiguousarray(dn.transpose(3, 0, 2, 1, 4)).reshape(4, 3, 128, 2048)
    w = np_("w_in_2")[0]
    cq, ckv, kr, qd, kd, vd, qi, ki, wi = np.split(w, np.cumsum([256, 128, 32, 512, 128, 128, 256, 32])[:8], axis=1)
    sw = np.concatenate([kr[:, 16:], kr[:, :16]], 1)
    qd = qd.reshape(1024, 2, 4, 64).transpose(0, 2, 1, 3).reshape(1024, 512)
    allc = np.concatenate([cq, ckv, kr, sw, kr, sw, qd, qi, ki, ki, ki, ki, kd], 1)
    o["w2in"] = pieces(allc)
    o["wv"] = pieces(np.concatenate([vd, wi], 1), 136)[0]
    qb = np_("w_q_b_2")[0].reshape(256, 8, 96)
    qb = np.concatenate([qb, qb[:, :, 80:96], qb[:, :, 64:80]], 2).reshape(256, 1024)
    o["qb"] = pieces(qb, 1024)[0]
    kvb = np_("w_kv_b_2")[0].reshape(128, 8, 2, 64).transpose(0, 2, 1, 3)
    o["kvb"] = np.ascontiguousarray(kvb).reshape(128, 1024)
    o["w_o"] = pieces(np_("w_o_2")[0])
    pos = np_("positions_2")[0]
    o["posr"] = np.ascontiguousarray(np.broadcast_to(pos[None], (128, 256)))
    o["posc"] = np.ascontiguousarray(pos.reshape(2, 128).T)
    o["wr"] = pieces(np_("w_router_2")[0], 32)[0]
    o["br"] = np.ascontiguousarray(np.broadcast_to(np_("b_router_2")[0][None], (128, 32)))
    o["b1"] = np.concatenate([np_("b_mlp1_2")[0]] * 3, 0)
    o["b2"] = np_("b_mlp2_2")[0]
    r = np.arange(96)[:, None] % 32 == np.arange(NE * CAP)[None, :] // CAP
    o["sel96"] = r.astype(np.float32)
    o["w_mlp1"] = np_("w_mlp1_2")[0]
    o["w_mlp2"] = np_("w_mlp2_2")[0]
    return o


def kernel(**inputs):
    import concourse.bacc as bacc
    from concourse.bass_utils import run_bass_kernel_spmd as launch

    nc = bacc.Bacc("TRN2", target_bir_lowering=False, num_devices=1)
    arrays, aps = {}, {}
    for name, v in lay_out(inputs).items():
        arrays["in_" + name] = v
        aps[name] = nc.dram_tensor("in_" + name, v.shape, mybir.dt.from_np(v.dtype), kind="ExternalInput").ap()
    o = nc.dram_tensor("out_xT", (128, 8, 256), F32, kind="ExternalOutput").ap()
    program(nc, aps, o)
    r = launch(nc, [arrays], core_ids=[0])
    y = r.results[0]["out_xT"]
    return np.ascontiguousarray(y.transpose(1, 0, 2).reshape(1024, 256).T)[None]
```

```python
from contextlib import ExitStack

import numpy as np

import concourse.bass as bass
from concourse import mybir

F32 = mybir.dt.float32
BF16 = mybir.dt.bfloat16
I32 = mybir.dt.int32
ALU = mybir.AluOpType
ACT = mybir.ActivationFunctionType
AX = mybir.AxisListType

S = 256
D = 1024
NK = 8
EPS = 1e-6
NEG = -1e30
NE = 32
CAP = 64
RING = 17
SLOT = 2048

COLS = {}


def _layout_cols():
    n = 0
    for name, w in (("c", 8), ("c2", 8), ("ada_b", 48), ("b_ada2", 48), ("norm1", 8), ("norm2", 8),
                    ("conv_w", 32), ("conv_b", 8), ("ba", 8), ("bx", 8), ("lam", 8), ("qg", 1), ("kg", 1),
                    ("fw", 144), ("fb", 48), ("pre_mix", 8), ("post_mix", 8), ("pre_ffn", 8),
                    ("post_ffn", 8), ("gq", 2), ("gkv", 1)):
        COLS[name] = (n, w)
        n += w
    return n


NCOL = _layout_cols()

CONST = {}


def _layout_consts():
    n = 0
    for name, w in (("ident", 128), ("ones", 128), ("nones", 128), ("negU", 128), ("uinc", 128), ("smask", 384),
                    ("sbias", 384), ("cbias", 384), ("iota", 256), ("freq", 1), ("sign", 1)):
        CONST[name] = (n, w)
        n += w
    return n


NCONST = _layout_consts()


def constants():
    c = np.zeros((128, NCONST), np.float32)

    def put(name, v):
        o, w = CONST[name]
        c[:, o:o + w] = v

    p = np.arange(128)[:, None]
    f = np.arange(128)[None, :]
    put("ident", (p == f).astype(np.float32))
    put("ones", 1.0)
    put("nones", -1.0)
    put("negU", -(p >= f).astype(np.float32))
    put("uinc", (p <= f).astype(np.float32))
    strict = (p < f).astype(np.float32)
    one = np.ones((128, 128), np.float32)
    m = np.concatenate([strict, one, strict], 1)
    put("smask", m)
    put("sbias", np.where(m > 0, 0.0, NEG))
    tri = np.where(f <= p, 0.0, NEG)
    put("cbias", np.concatenate([tri, 0 * one, tri], 1))
    put("iota", np.concatenate([f % 64, 64 + f % 64], 1).astype(np.float32) * np.ones((128, 1)))
    half = 16
    fr = np.float32(10000.0) ** (-np.arange(half, dtype=np.float32) / np.float32(half))
    put("freq", fr[p % half].astype(np.float32))
    put("sign", np.where((p % 32) < 16, -1.0, 1.0))
    return c


def two_pi_parts():
    rest = 2.0 * np.pi
    parts = []
    for _ in range(4):
        e = np.floor(np.log2(rest))
        q = 2.0 ** (e - 11)
        v = np.floor(rest / q) * q
        parts.append(float(v))
        rest -= v
    return parts


class Prog:

    ENGINES = ("pe", "act", "dve", "pool", "sp")

    def __init__(self, me, eng, semaphore):
        self.me, self.eng, self.semaphore = me, eng, semaphore
        self.new_semaphores("")

    def new_semaphores(self, suffix):
        self.sem = {e: self.semaphore("s_" + e + suffix) for e in self.ENGINES}
        self.restart()

    def restart(self):
        self.cnt = {e: 0 for e in self.ENGINES}
        self.seen = {}

    def wait(self, eng, *tokens):
        if eng != self.me:
            return
        for t in _flat(tokens):
            sem, val = (self.sem[t[0]], t[1]) if isinstance(t[0], str) else t
            if self.seen.get(id(sem), 0) < val:
                self.seen[id(sem)] = val
                self.eng.wait_ge(sem, val)

    def op(self, eng, fn, *tokens, inc=True):
        self.wait(eng, *tokens)
        if inc:
            self.cnt[eng] += 1
        if eng == self.me:
            made = fn(self.eng)
            if inc:
                made.then_inc(self.sem[eng], 1)
        return (eng, self.cnt[eng]) if inc else None

    def dma(self, eng, fn, sem, *tokens):
        self.wait(eng, *tokens)
        if eng == self.me:
            fn(self.eng).then_inc(sem, 16)

    def last(self, eng):
        return (eng, self.cnt[eng]) if self.cnt[eng] else None

    def begin_if(self, engines, taken):
        self.engines, self.before, self.saw = engines, dict(self.cnt), dict(self.seen)
        self.branch = ExitStack()
        if self.me in engines:
            self.branch.enter_context(self.eng.If(taken))
        self.full = None

    def begin_else(self):
        self.branch.close()
        self.full = self.cnt
        self.cnt, self.seen = dict(self.before), dict(self.saw)
        self.branch = ExitStack()
        if self.me in self.engines:
            self.branch.enter_context(self.eng.Else())

    def end_if(self):
        if self.full is None:
            self.begin_else()
        if self.me in self.engines and self.full[self.me] > self.cnt[self.me]:
            self.eng.wait_ge(self.sem[self.me], self.cnt[self.me])
            self.eng.sem_inc(self.sem[self.me], self.full[self.me] - self.cnt[self.me])
        self.branch.close()
        self.cnt, self.seen = self.full, self.saw

    def begin_loop(self, engines, load):
        self.restart()
        self.rounds = ExitStack()
        if self.me in engines:
            self.rounds.enter_context(self.eng.While(lambda: load(self.eng) > 0))

    def end_loop(self, load, clear, bar, go, again):
        if self.me == "sp":
            self.eng.wait_ge(bar, len(go))
            for s in clear:
                self.eng.sem_clear(s)
            self.eng.sem_clear(bar)
            with self.eng.If(load(self.eng) > 0):
                for dst, src, sem in again:
                    self.eng.dma_start(dst, src).then_inc(sem, 16)
            for s in go.values():
                self.eng.sem_inc(s, 1)
        elif self.me in go:
            self.eng.wait_ge(self.sem[self.me], self.cnt[self.me])
            self.eng.sem_inc(bar, 1)
            self.eng.wait_ge(go[self.me], 1)
            self.eng.sem_clear(go[self.me])
        self.rounds.close()
        self.restart()


def _flat(x):
    for t in x:
        if t is None:
            continue
        if isinstance(t, tuple):
            yield t
        else:
            yield from _flat(t)


def program(nc, a, out, stage=99):
    with ExitStack() as ctx:
        made = {}

        def sb(name, shape, dt=F32):
            if name not in made:
                made[name] = ctx.enter_context(nc.sbuf_tensor(name, shape, dt))
            return made[name]

        def psum(name):
            if name not in made:
                made[name] = ctx.enter_context(nc.psum_tensor(name, [128, 512], F32))
            return made[name]

        def sem(name):
            if name not in made:
                made[name] = ctx.enter_context(nc.semaphore(name))
            return made[name]

        walk(None, None, a, out, sb, psum, sem)
        block = ctx.enter_context(nc.Block())
        block.sync(lambda e: walk("sp", e, a, out, sb, psum, sem))
        block.tensor(lambda e: walk("pe", e, a, out, sb, psum, sem))
        block.scalar(lambda e: walk("act", e, a, out, sb, psum, sem))
        block.vector(lambda e: walk("dve", e, a, out, sb, psum, sem))
        block.gpsimd(lambda e: walk("pool", e, a, out, sb, psum, sem))


def walk(me, eng, a, out, sb, psum, sem):
        P = Prog(me, eng, sem)

        serial = [False]

        def V(fn, *w):
            return P.op("dve", fn, P.last("dve") if serial[0] else None, *w)

        def A(fn, *w):
            return P.op("act", fn, *w)

        def G(fn, *w):
            return P.op("pool", fn, *w)

        def T(fn, *w, inc=False):
            return P.op("pe", fn, *w, inc=inc)

        ring = sb("ring", [128, RING, SLOT])
        con = sb("con", [128, NCONST])
        col = sb("col", [128, NCOL])
        modc = sb("modc", [128, 2, 48])
        mc = sb("mc", [128, 48])
        xT = sb("xT", [128, 8, 256])
        hT = sb("hT", [128, 8, 256])
        SCN = 14700
        scr = sb("scr", [128, SCN])
        B = [psum(f"bank{i}") for i in range(8)]

        def K(name, a0=0, a1=None):
            o, w = CONST[name]
            return con[:, o + a0:o + (w if a1 is None else a1)]

        def C(name, i=0, n=1):
            o, w = COLS[name]
            return col[:, o + i:o + i + n]

        used = [0]

        def carve(*dims):
            n = int(np.prod(dims))
            o = used[0]
            used[0] += n
            assert used[0] <= top[0], (used[0], top[0])
            v = scr[:, o:o + n]
            if len(dims) == 2:
                v = v.rearrange("p (a b) -> p a b", a=dims[0])
            if len(dims) == 3:
                v = v.rearrange("p (a b c) -> p a b c", a=dims[0], b=dims[1])
            return v

        top = [SCN]

        def carve_top(n):
            top[0] -= n
            return scr[:, top[0]:top[0] + n]

        def fence():
            every = [P.last(e) for e in ("pe", "act", "dve", "pool")]
            for e in ("pe", "act", "dve", "pool"):
                P.wait(e, *every)
            used[0] = 0

        freed = {i: None for i in range(8)}
        turn = [0]
        pool_banks = [list(range(7))]

        def bank():
            lst = pool_banks[0]
            i = lst[turn[0] % len(lst)]
            turn[0] += 1
            return i, B[i], freed[i]

        slot_sem = [sem(f"w{i}") for i in range(RING)]
        slot_use = [0] * RING
        slot_free = [None] * RING
        piece = [0]

        def slot_view(s, src, n):
            dst = ring[0:src.shape[0], s, 0:n]
            if len(src.shape) == 3:
                dst = dst.rearrange("p (a b) -> p a b", a=src.shape[1])
            return dst

        def load(src, n=SLOT):
            s = piece[0] % RING
            piece[0] += 1
            assert slot_free[s] is not False
            slot_use[s] += 16
            dst = slot_view(s, src, n)
            P.dma("sp", lambda e: e.dma_start(dst, src), slot_sem[s], slot_free[s])
            slot_free[s] = False
            return s, ring[:, s, 0:n], (slot_sem[s], slot_use[s])

        def done(s, token):
            slot_free[s] = token

        s_small = [sem(f"small{i}") for i in range(8)]
        P.dma("act", lambda e: e.dma_start(col[:, :], a["cols"]), s_small[0])
        P.dma("act", lambda e: e.dma_start(con[:, 0:256], a["consts"][:, 0:256]), s_small[1])
        P.dma("act", lambda e: e.dma_start(xT[:, :, :], a["xT"]), s_small[2])
        t_col, t_con, t_x = (s_small[0], 16), (s_small[1], 16), (s_small[2], 16)

        eps = sb("eps", [128, 1])
        onec = sb("onec", [128, 2])
        t_eps = V(lambda e: e.memset(eps[:, :], EPS))
        t_eps = V(lambda e: e.memset(onec[:, 0:1], 1.0))
        t_eps = [t_eps, ("dve", 1)]

        def rms(src, n, dim, sq, rst, width, *w):
            flat = src.rearrange("p a b -> p (a b)") if n > 1 else src
            sqf = sq.rearrange("p a b -> p (a b)") if n > 1 else sq
            t = A(lambda e: e.activation(sqf, flat, ACT.Square), *w)
            i, b, fr = bank()
            for k in range(n):
                rk = sq[:, k, :] if n > 1 else sq
                tt = T(lambda e, k=k, rk=rk: e.matmul(b[:, 0:width], K("ones"), rk, start=(k == 0), stop=(k == n - 1)),
                       t, fr, t_con, inc=(k == n - 1))
            t = A(lambda e: e.activation(rst, b[:, 0:width], ACT.Sqrt, bias=eps[:, 0:1], scale=1.0 / dim), tt, t_eps)
            freed[i] = t
            return V(lambda e: e.reciprocal(rst, rst), t)

        crep = sb("crep", [128, 8, 32])
        rowsb = sb("rowsb", [128, 512])
        t_rows = [None]

        def make_crep(src, *w):
            v = None
            for k in range(8):
                v = V(lambda e, k=k: e.tensor_scalar(crep[:, k, :], K("ones", 0, 32), src[:, k:k + 1], None, ALU.mult),
                      t_con, t_col, P.last("pe"), *w)
            return v

        def ada(w_dram, g, blk, bias, t_c):
            i, b, fr = bank()
            for k in range(8):
                s, v, tl = load(w_dram[k * 128:(k + 1) * 128, g * 2048:(g + 1) * 2048])
                for j in range(4):
                    t = T(lambda e, k=k, j=j, v=v: e.matmul(b[32 * j:32 * j + 32, :], crep[:, k, :],
                                                            v[:, 512 * j:512 * j + 512], start=(k == 0), stop=(k == 7)),
                          tl, fr, t_c, inc=(j == 3))
                done(s, t)
            t = A(lambda e: e.activation(rowsb[:, :], b[:, :], ACT.Copy), t, t_rows[0])
            freed[i] = t
            i, b2, fr = bank()
            for q in range(4):
                tt = T(lambda e, q=q: e.transpose(b2[:, q * 128:(q + 1) * 128], rowsb[:, q * 128:(q + 1) * 128],
                                                  K("ident")), t, fr, inc=(q == 3))
            t_rows[0] = tt
            src = b2[:, :].rearrange("p (b j r) -> p b j r", b=4, r=32)[:, :, :, 0]
            dst = modc[:, blk, g * 16:g * 16 + 16].rearrange("p (j b) -> p b j", b=4)
            t = V(lambda e: e.tensor_copy(dst, src), tt)
            freed[i] = t
            return V(lambda e: e.tensor_tensor(modc[:, blk, g * 16:g * 16 + 16], modc[:, blk, g * 16:g * 16 + 16],
                                               C(bias, g * 16, 16), ALU.add), t, t_col)

        def modulate(blk, which, gname, rst, *w):
            sh, sc = which * 8, which * 8 + 8
            t1 = V(lambda e: e.scalar_tensor_tensor(mc[:, 0:8], modc[:, blk, sc:sc + 8], 1.0, C(gname, 0, 8), ALU.add,
                                                    ALU.mult), *w)
            o = []
            for k in range(8):
                t2 = V(lambda e, k=k: e.tensor_tensor(hT[:, k, :], xT[:, k, :], rst, ALU.mult), *w)
                o.append(A(lambda e, k=k: e.activation(hT[:, k, :], hT[:, k, :], ACT.Identity,
                                                       bias=modc[:, blk, sh + k:sh + k + 1],
                                                       scale=mc[:, k:k + 1]), t1, t2))
            return o

        norm = {"n": 0}

        def norm_square(c, sq, *w, src=xT):
            src = src[:, 2 * c:2 * c + 2, :].rearrange("p a b -> p (a b)")
            norm[c] = (sq, A(lambda e: e.activation(sq, src, ACT.Square), *w))

        def norm_sum(c):
            sq, t = norm[c]
            for j in range(2):
                norm["t"] = T(lambda e: e.matmul(B[7][:, 0:256], K("ones"), sq[:, 256 * j:256 * j + 256],
                                                 start=(c == 0 and j == 0), stop=(c == 3 and j == 1)),
                              t, freed[7], t_con, inc=(j == 1))
            return norm["t"]

        def norm_end(rst):
            t = A(lambda e: e.activation(rst, B[7][:, 0:256], ACT.Sqrt, bias=eps[:, 0:1], scale=1.0 / D), norm["t"],
                  t_eps)
            freed[7] = t
            return V(lambda e: e.reciprocal(rst, rst), t)

        def sqrt_table():
            A(lambda e: e.activation(onec[:, 1:2], eps[:, 0:1], ACT.Sqrt), t_eps, P.last("act"))

        def tiles2(v, rhs, w, kn=8, b=None, fr=None):
            for j in range(2):
                for k in range(kn):
                    t = T(lambda e, j=j, k=k: e.matmul(b[:, 256 * j:256 * j + 256],
                                                       v[:, k * 256 + j * 128:k * 256 + j * 128 + 128],
                                                       rhs[:, k, :], start=(k == 0), stop=(k == kn - 1)),
                          fr, w[0], w[1][k] if len(w[1]) == kn else w[1], inc=(j == 1 and k == kn - 1))
            return t

        t_c = make_crep(C("c", 0, 8))
        lt = [carve(8) for _ in range(6)]
        t = A(lambda e: e.activation(lt[0], C("lam", 0, 8), ACT.Abs), t_col)
        t = A(lambda e: e.activation(lt[0], lt[0], ACT.Exp, scale=-1.0), t)
        t = V(lambda e: e.tensor_scalar(lt[1], lt[0], 2.0, None, ALU.add), t)
        t = V(lambda e: e.reciprocal(lt[1], lt[1]), t)
        t = V(lambda e: e.tensor_tensor(lt[1], lt[1], lt[0], ALU.mult), t)
        t = V(lambda e: e.tensor_tensor(lt[2], lt[1], lt[1], ALU.mult), t)
        t = V(lambda e: e.tensor_scalar(lt[3], lt[2], 1.0 / 19.0, 1.0 / 17.0, ALU.mult, ALU.add), t)
        for n in range(15, 0, -2):
            t = V(lambda e: e.tensor_tensor(lt[3], lt[3], lt[2], ALU.mult), t)
            t = V(lambda e, n=n: e.tensor_scalar(lt[3], lt[3], 1.0 / n, None, ALU.add), t)
        t = V(lambda e: e.scalar_tensor_tensor(lt[3], lt[3], 2.0, lt[1], ALU.mult, ALU.mult), t)
        t = V(lambda e: e.tensor_scalar(lt[4], C("lam", 0, 8), -1.0, 0.0, ALU.mult, ALU.max), t)
        t = V(lambda e: e.tensor_tensor(lt[3], lt[3], lt[4], ALU.add), t)
        sp8 = sb("sp8", [128, 16])
        t_sp = V(lambda e: e.tensor_scalar(sp8[:, 0:8], lt[3], 8.0, None, ALU.mult), t)
        t_sp = V(lambda e: e.tensor_scalar(sp8[:, 8:16], lt[3], -8.0, None, ALU.mult), t)
        hb = sb("hb", [128, 16])
        t_hb = V(lambda e: e.tensor_scalar(hb[:, 0:8], C("ba", 0, 8), 0.5, None, ALU.mult), t_col)
        t_hb = V(lambda e: e.tensor_scalar(hb[:, 8:16], C("bx", 0, 8), 0.5, None, ALU.mult), t_col)

        sqs = [carve(512) for _ in range(4)]
        rst = carve(256)
        for c in range(4):
            norm_square(c, sqs[c], t_x)
        for c in range(4):
            norm_sum(c)
        t_r = norm_end(rst)
        t_m = ada(a["ada_w"], 0, 0, "ada_b", t_c)
        P.dma("sp", lambda e: e.dma_start(con[:, 256:NCONST], a["consts"][:, 256:NCONST]), s_small[3])
        t_h = modulate(0, 0, "norm1", rst, t_m, t_r)
        used[0] = 0

        qk = [carve(8, 256), carve(8, 256)]
        vv = carve(2, 1024)
        mix = carve(8, 256)
        Wt = [carve(512) for _ in range(10)]
        xp = carve(2, 260)

        def w_in(ci):
            s, v, tl = load(a["w_in"][ci])
            return s, v, tl

        def t_tile_chunk(ci):
            s, v, tl = w_in(ci)
            i, b, fr = bank()
            t = tiles2(v, hT, [tl, t_h], b=b, fr=fr)
            done(s, t)
            return i, b, t

        for e_ in ("pe", "act", "dve"):
            P.wait(e_, (s_small[3], 16))

        def qk_tile(which, c):
            i, b, t = t_tile_chunk((8, 12)[which] + c)
            dst = qk[which][:, 2 * c:2 * c + 2, :].rearrange("p a b -> p (a b)")
            t1 = V(lambda e: e.tensor_copy(dst, b[:, :]), t, t_h)
            freed[i] = t1
            sq = Wt[2 * (c % 2)]
            return which, dst, sq, Wt[2 * (c % 2) + 1], t1, A(lambda e: e.activation(sq, dst, ACT.Square), t1,
                                                               P.last("pe"), t_r)

        def qk_norm(which, dst, sq, rst_, t1, t2):
            i, b, fr = bank()
            t = T(lambda e: e.matmul(b[:, :], K("ones"), sq, start=True, stop=True), t2, fr, inc=True)
            t = A(lambda e: e.activation(rst_, b[:, :], ACT.Sqrt, bias=eps[:, 0:1], scale=1.0 / 128), t,
                  P.last("dve"))
            freed[i] = t
            t = V(lambda e: e.reciprocal(rst_, rst_), t)
            t = V(lambda e: e.scalar_tensor_tensor(dst, dst, C("kg" if which else "qg"), rst_, ALU.mult, ALU.mult),
                  t1, t)
            if which == 0:
                t = V(lambda e: e.tensor_scalar(dst, dst, 128.0 ** -0.5, None, ALU.mult), t)
            return t

        before = None
        for n in range(8):
            now = qk_tile(n // 4, n % 4)
            if before:
                t_k = qk_norm(*before)
            before = now
            if n == 4:
                t_q = t_k

        def v_tile(c):
            s, v, tl = w_in(16 + c)
            i, b, fr = bank()
            for tt in range(2):
                for k in range(8):
                    t = T(lambda e, tt=tt, k=k: e.matmul(b[:, 256 * tt:256 * tt + 256],
                                                         hT[:, k, tt * 128:(tt + 1) * 128],
                                                         v[:, k * 256:(k + 1) * 256], start=(k == 0), stop=(k == 7)),
                          fr, tl, t_h, inc=(tt == 1 and k == 7))
            done(s, t)
            t_v = A(lambda e, c=c: e.activation(vv[:, :, 256 * c:256 * c + 256],
                                                b[:, :].rearrange("p (a b) -> p a b", a=2), ACT.Copy), t)
            freed[i] = t_v
            return t_v

        t_pad = V(lambda e: e.memset(xp[:, :, 0:3], 0.0))

        att = {}

        def att1(h):
            i, b, fr = bank()
            q, k = qk[0][:, h, :], qk[1][:, h, :]
            T(lambda e: e.matmul(b[:, 0:256], k[:, 0:128], q, start=True, stop=False, skip_group_check=True),
              fr, t_q, t_k)
            t = T(lambda e: e.matmul(b[:, 256:384], k[:, 128:256], q[:, 128:256], start=False, stop=False,
                                     skip_group_check=True), inc=True)
            w0, w1 = Wt[8][:, 0:384], Wt[9][:, 0:384]
            t1 = A(lambda e: e.activation(w0, b[:, 0:384], ACT.Abs), t, P.last("dve"), P.last("pe"))
            t1 = A(lambda e: e.activation(w0, w0, ACT.Exp, scale=-1.0), t1)
            t1 = A(lambda e: e.activation(w0, w0, ACT.Ln, bias=onec[:, 0:1]), t1)
            t1 = V(lambda e: e.scalar_tensor_tensor(w1, b[:, 0:384], 0.0, w0, ALU.max, ALU.add), t1, P.last("pe"))
            t1 = V(lambda e: e.tensor_tensor(w1, w1, K("smask"), ALU.mult), t1)
            att[h] = (i, b, t1)

        def att2(h):
            i, b, t1 = att[h]
            w0, w1 = Wt[8][:, 0:384], Wt[9][:, 0:384]
            T(lambda e: e.matmul(b[:, 0:384], K("negU"), w1, start=False, stop=False, skip_group_check=True), t1)
            t = T(lambda e: e.matmul(b[:, 128:256], K("nones"), w1[:, 256:384], start=False, stop=True,
                                     skip_group_check=True), inc=True)
            t1 = V(lambda e: e.tensor_tensor(w0, b[:, 0:384], K("sbias"), ALU.add), t, P.last("act"))
            freed[i] = t1
            t1 = A(lambda e: e.activation(w0, w0, ACT.Exp), t1)
            att[h] = t1

        def att3(h):
            w0 = Wt[8][:, 0:384]
            i, b, fr = bank()
            T(lambda e: e.matmul(b[:, 0:256], vv[:, 0, h * 128:(h + 1) * 128], w0[:, 0:256], start=True, stop=False,
                                 skip_group_check=True), fr, att[h], t_vs[h // 2])
            t = T(lambda e: e.matmul(b[:, 128:256], vv[:, 1, h * 128:(h + 1) * 128], w0[:, 256:384], start=False,
                                     stop=True, skip_group_check=True), inc=True)
            t1 = V(lambda e: e.tensor_copy(qk[0][:, h, :], b[:, 0:256]), t)
            freed[i] = t1
            att[h] = t1

        def step(n):
            if n % 2 == 0:
                if n >= 2:
                    att3(n // 2 - 1)
                if n < 16:
                    att1(n // 2)
            else:
                att2(n // 2)

        def mixv(c):
            return mix[:, 2 * c:2 * c + 2, :].rearrange("p a b -> p (a b)")

        nstep = 0
        t_mix = {}
        t_k = qk_norm(*before)
        t_vs, t_gels = [], []
        xcs = [Wt[0], carve(512)]

        def conv(c, t_xp):
            i, b, t = t_tile_chunk(c)
            w = P.last("pe")
            t1 = A(lambda e: e.activation(xp[:, :, 3:259], b[:, :].rearrange("p (a b) -> p a b", a=2), ACT.Copy), t,
                   t_pad, t_xp)
            freed[i] = t1
            for j in range(2):
                tl_ = 2 * c + j
                xc = xcs[c % 2][:, 256 * j:256 * j + 256]
                t2 = V(lambda e, j=j, xc=xc, tl_=tl_: e.tensor_scalar(xc, xp[:, j, 3:259], C("conv_w", 24 + tl_),
                                                                      C("conv_b", tl_), ALU.mult, ALU.add), t1, w)
                for k in (2, 1, 0):
                    t2 = V(lambda e, j=j, xc=xc, tl_=tl_, k=k: e.scalar_tensor_tensor(
                        xc, xp[:, j, k:k + 256], C("conv_w", 8 * k + tl_), xc, ALU.mult, ALU.add), t2)
            return t2

        t2 = conv(0, P.last("dve"))
        for c in range(4):
            xc = xcs[c % 2]
            t_vs.append(v_tile(c))
            i, b, t = t_tile_chunk(4 + c)
            gel = Wt[6 + c % 2]
            t_gel = A(lambda e, gel=gel: e.activation(gel, b[:, :], ACT.Gelu_apprx_tanh), t, t_gels[c - 2:c - 1])
            freed[i] = t_gel
            step(nstep)
            t_xc = t2
            if c < 3:
                t2 = conv(c + 1, t2)
            step(nstep + 1)
            nstep += 2
            s_rg, rg, t_rg = load(a["rg"][c], 512)
            ir, br, fr = bank()
            ii, bi, fi = bank()
            for j in range(2):
                T(lambda e, j=j: e.matmul(br[:, 256 * j:256 * j + 256], rg[:, j * 128:(j + 1) * 128],
                                          xc[:, 256 * j:256 * j + 256], start=True, stop=True), fr, t_xc, t_rg)
                t = T(lambda e, j=j: e.matmul(bi[:, 256 * j:256 * j + 256],
                                              rg[:, 256 + j * 128:256 + (j + 1) * 128],
                                              xc[:, 256 * j:256 * j + 256], start=True, stop=True), fi, inc=True)
            done(s_rg, t)
            for j in range(2):
                tl_ = 2 * c + j
                sl = slice(256 * j, 256 * j + 256)
                t3 = A(lambda e, sl=sl, tl_=tl_: e.activation(Wt[1][:, sl], br[:, sl], ACT.Tanh, scale=0.5,
                                                              bias=hb[:, tl_:tl_ + 1]), t, t_hb, P.last("dve"))
                t4 = A(lambda e, sl=sl, tl_=tl_: e.activation(Wt[2][:, sl], bi[:, sl], ACT.Tanh, scale=0.5,
                                                              bias=hb[:, 8 + tl_:9 + tl_]))
            freed[ir], freed[ii] = t3, t4
            t3 = V(lambda e: e.tensor_scalar(Wt[1], Wt[1], 0.5, 0.5, ALU.mult, ALU.add), t3)
            t4 = V(lambda e: e.tensor_scalar(Wt[2], Wt[2], 0.5, 0.5, ALU.mult, ALU.add), t4)
            for j in range(2):
                tl_ = 2 * c + j
                sl = slice(256 * j, 256 * j + 256)
                t5 = A(lambda e, sl=sl, tl_=tl_: e.activation(Wt[3][:, sl], Wt[1][:, sl], ACT.Tanh,
                                                              scale=sp8[:, tl_:tl_ + 1]), t3, t_sp)
                t6 = A(lambda e, sl=sl, tl_=tl_: e.activation(Wt[4][:, sl], Wt[1][:, sl], ACT.Exp,
                                                              scale=sp8[:, 8 + tl_:9 + tl_]), t3)
            t7 = V(lambda e: e.tensor_scalar(Wt[5], Wt[3], 1.0, None, ALU.add), t5)
            t7 = V(lambda e: e.reciprocal(Wt[5], Wt[5]), t7)
            t7 = V(lambda e: e.scalar_tensor_tensor(Wt[3], Wt[3], 2.0, Wt[5], ALU.mult, ALU.mult), t7)
            t7 = A(lambda e: e.activation(Wt[3], Wt[3], ACT.Sqrt), t7)
            t8 = V(lambda e: e.tensor_tensor(Wt[2], Wt[2], xc, ALU.mult), t4)
            t8 = V(lambda e: e.tensor_tensor(Wt[2], Wt[2], Wt[3], ALU.mult), t8, t7)
            for j in range(2):
                t9 = V(lambda e, j=j: e.tensor_tensor_scan(mix[:, 2 * c + j, :], Wt[4][:, 256 * j:256 * j + 256],
                                                           Wt[2][:, 256 * j:256 * j + 256], 0.0, ALU.mult, ALU.add),
                       t8, t6)
            t_mix[c] = V(lambda e, gel=gel, c=c: e.tensor_tensor(mixv(c), mixv(c), gel, ALU.mult), t_gel, t9)
            t_gels.append(t_mix[c])
        for c in range(4):
            i, b, t = t_tile_chunk(20 + c)
            step(nstep)
            nstep += 1
            wt = Wt[2 + c % 2]
            t1 = A(lambda e, wt=wt: e.activation(wt, b[:, :], ACT.Sigmoid), t, P.last("dve"))
            freed[i] = t1
            t_mix[c] = V(lambda e, wt=wt, c=c: e.tensor_tensor(mixv(c), mixv(c), wt, ALU.mult), t1, t_mix[c])
        gate_b = []
        for c in range(4):
            i, b, t = t_tile_chunk(24 + c)
            step(nstep)
            nstep += 1
            wt = Wt[4 + c]
            t1 = A(lambda e, wt=wt: e.activation(wt, b[:, :], ACT.Sigmoid), t, P.last("dve"))
            freed[i] = t1
            gate_b.append((wt, t1))
        step(16)
        for c in range(4):
            wt, t1 = gate_b[c]
            yq = qk[0][:, 2 * c:2 * c + 2, :].rearrange("p a b -> p (a b)")
            t1 = V(lambda e, wt=wt, yq=yq: e.tensor_tensor(wt, wt, yq, ALU.mult), t1, att[2 * c], att[2 * c + 1])
            t_mix[c] = V(lambda e, wt=wt, c=c: e.tensor_tensor(mixv(c), mixv(c), wt, ALU.add), t1, t_mix[c])
        t_m1 = ada(a["ada_w"], 1, 0, "ada_b", t_c)
        t_m2 = ada(a["ada_w"], 2, 0, "ada_b", t_c)

        def project_add(w, src, t_src, blk, gate, sqs):
            o = []
            sqrt_table()
            for c in range(4):
                s, v, tl = load(w[c])
                i, b, fr = bank()
                t = tiles2(v, src, [tl, t_src], b=b, fr=fr)
                done(s, t)
                for j in range(2):
                    n = 2 * c + j
                    o.append(V(lambda e, j=j, n=n, b=b: e.scalar_tensor_tensor(
                        xT[:, n, :], b[:, 256 * j:256 * j + 256], modc[:, blk, gate + n:gate + n + 1], xT[:, n, :],
                        ALU.mult, ALU.add), t))
                freed[i] = o[-1]
                norm_square(c, sqs[c % 2], o[-1], o[-2], P.last("pe"), P.last("dve"))
                if c:
                    norm_sum(c - 1)
            norm_sum(3)
            return o

        P.wait("dve", t_m1, t_m2)
        t_x1 = project_add(a["w_out"], mix, [t_mix[c] for c in range(4)], 0, 16, [Wt[0], Wt[1]])
        fence()
        rst = rowsb[:, 0:256]
        t_r = norm_end(rst)
        t_h = modulate(0, 3, "norm2", rst, t_r)

        sl2 = sb("sl2", [128, 8])
        t = A(lambda e: e.activation(sl2[:, :], C("c2", 0, 8), ACT.Sigmoid), t_col)
        t = V(lambda e: e.tensor_tensor(sl2[:, :], sl2[:, :], C("c2", 0, 8), ALU.mult), t)
        t_crep = make_crep(sl2, t)
        ff = carve(24, 256)
        ub = [carve(2, 260) for _ in range(3)]
        cv = [carve(2, 256) for _ in range(3)]
        t_z = [V(lambda e, n=n: e.memset(ub[n][:, :, 0:2], 0.0)) for n in range(3)]
        t_cv = [None] * 3
        t_ff = None
        brt = sb("brt", [128, 32])
        s_p = [sem(f"p{n}") for n in range(8)]
        b1h = carve_top(1024)[0:96].bitcast(BF16)
        sel96_f = carve_top(16)[0:96]
        sel96 = sel96_f.bitcast(BF16)
        cs, dist = carve_top(256), carve_top(384)
        W = [carve(512) for _ in range(6)]
        posr = W[5][:, 0:256].bitcast(I32)
        posc = carve(2).bitcast(I32)
        pi = W[4].bitcast(I32).rearrange("p (a b) -> p a b", a=2)
        pci = carve(2, 2).bitcast(I32)
        pcf = carve(2, 2)
        at = [P.last("dve"), P.last("act"), P.last("pe")]
        P.dma("act", lambda e: e.dma_start(posr, a["posr"]), s_p[0], at)
        P.dma("act", lambda e: e.dma_start(posc, a["posc"]), s_p[1], at)
        P.dma("act", lambda e: e.dma_start(sel96_f, a["sel96"]), s_p[3], at)
        P.dma("act", lambda e: e.dma_start(brt[:, :], a["br"]), s_p[2])
        t_s96 = (s_p[3], 16)
        got = {}

        def side_work():
            phi, plo = W[0][:, 0:256], W[0][:, 256:512]
            t = V(lambda e: e.tensor_single_scalar(pi[:, 0, :], posr, 12, ALU.arith_shift_right), (s_p[0], 16))
            t = V(lambda e: e.tensor_single_scalar(pi[:, 1, :], posr, 4095, ALU.bitwise_and), t)
            t1 = V(lambda e: e.tensor_single_scalar(pci[:, 0, :], posc, 12, ALU.arith_shift_right), (s_p[1], 16))
            t1 = V(lambda e: e.tensor_single_scalar(pci[:, 1, :], posc, 4095, ALU.bitwise_and), t1)
            t = V(lambda e: e.tensor_copy(phi, pi[:, 0, :]), t)
            t = V(lambda e: e.tensor_copy(plo, pi[:, 1, :]), t)
            t1 = V(lambda e: e.tensor_copy(pcf[:, :, :], pci[:, :, :]), t1)
            for tt, o0, w in ((0, 0, 128), (1, 128, 256)):
                d = dist[:, o0:o0 + w]
                t2 = V(lambda e: e.tensor_scalar(d, phi[:, 0:w], pcf[:, 0, tt:tt + 1], 4096.0, ALU.subtract, ALU.mult),
                       t, t1)
                t3 = V(lambda e: e.tensor_scalar(W[1][:, 0:w], plo[:, 0:w], pcf[:, 1, tt:tt + 1], None, ALU.subtract),
                       t, t1)
                t2 = V(lambda e: e.tensor_tensor(d, d, W[1][:, 0:w], ALU.add), t2, t3)
                t_dist = V(lambda e: e.scalar_tensor_tensor(d, d, -1.0, d, ALU.mult, ALU.max))
                yield
            ang, r1, r2 = W[2][:, 0:256], W[2][:, 256:512], W[3][:, 0:256]
            r3 = W[3][:, 256:512]
            TP = two_pi_parts()
            t = V(lambda e: e.scalar_tensor_tensor(ang, phi, 4096.0, plo, ALU.mult, ALU.add), t)
            t = V(lambda e: e.tensor_scalar(ang, ang, K("freq"), None, ALU.mult), t, t_con)
            for _ in range(2):
                t = V(lambda e: e.tensor_scalar(r1, ang, 1.0 / (2.0 * np.pi), None, ALU.mult), t)
                t = V(lambda e: e.tensor_copy(pi[:, 0, :], r1), t)
                t = V(lambda e: e.tensor_copy(r1, pi[:, 0, :]), t)
                t = V(lambda e: e.tensor_single_scalar(r2.bitcast(I32), r1.bitcast(I32), -4096, ALU.bitwise_and), t)
                t = V(lambda e: e.tensor_tensor(r3, r1, r2, ALU.subtract), t)
                yield
                for part in TP:
                    for r in (r2, r3):
                        t = V(lambda e: e.scalar_tensor_tensor(ang, r, -part, ang, ALU.mult, ALU.add), t)
            yield
            for sgn, cmp_ in ((-1.0, ALU.is_gt), (1.0, ALU.is_lt)):
                t = V(lambda e: e.tensor_scalar(r1, ang, -sgn * np.pi, sgn * 2.0 * np.pi, cmp_, ALU.mult), t)
                t = V(lambda e: e.tensor_tensor(ang, ang, r1, ALU.add), t)
            yield
            pi32 = float(np.nextafter(np.float32(np.pi), np.float32(0)))
            t = V(lambda e: e.tensor_scalar(ang, ang, pi32, -pi32, ALU.min, ALU.max), t)
            halfpi = sb("halfpi", [128, 1])
            t1 = V(lambda e: e.memset(halfpi[:, :], np.pi / 2))
            t2 = A(lambda e: e.activation(r1[64:96, :], ang[64:96, :], ACT.Abs), t)
            t2 = A(lambda e: e.activation(cs[64:96, :], r1[64:96, :], ACT.Sin, scale=-1.0, bias=halfpi[64:96, 0:1]),
                   t2, t1)
            t3 = A(lambda e: e.activation(cs[96:128, :], ang[96:128, :], ACT.Sin), t)
            t_cs = V(lambda e: e.tensor_scalar(cs[96:128, :], cs[96:128, :], K("sign")[96:128, :], None, ALU.mult), t3)
            got["cs"] = [t_cs, t2]
            got["dist"] = t_dist

            t = None
            for q in range(4):
                yield
                s_b1, vb1, tl = load(a["b1"][:, q * 512:(q + 1) * 512], 512)
                src = vb1[0:96, :]
                fb, ff_ = W[0][0:96, :], W[1][0:96, :]
                hb16 = W[2][0:96, 0:256].bitcast(BF16)
                dst = b1h[:, q * 512:(q + 1) * 512]
                t = V(lambda e: e.tensor_copy(hb16, src), t, tl)
                t = V(lambda e: e.tensor_copy(dst[0:32], hb16[0:32]), t)
                yield
                t = V(lambda e: e.tensor_copy(fb, hb16), t)
                t = V(lambda e: e.tensor_tensor(ff_, src, fb, ALU.subtract), t)
                yield
                t = V(lambda e: e.tensor_copy(hb16, ff_), t)
                t = V(lambda e: e.tensor_copy(dst[32:64], hb16[32:64]), t)
                t = V(lambda e: e.tensor_copy(fb, hb16), t)
                t = V(lambda e: e.tensor_tensor(ff_, ff_, fb, ALU.subtract), t)
                t = V(lambda e: e.tensor_copy(dst[64:96], ff_[64:96]), t)
                done(s_b1, t)
            got["b1"] = t

        side = side_work()

        def some():
            serial[0] = True
            more = next(side, False) is not False
            serial[0] = False
            return more

        for j in range(24):
            s, v, tl = load(a["up"][j])
            i, b, fr = bank()
            t = tiles2(v, hT, [tl, t_h], b=b, fr=fr)
            done(s, t)
            u, w = ub[j % 3], cv[j % 3]
            t1 = A(lambda e, u=u, b=b: e.activation(u[:, :, 2:258], b[:, :].rearrange("p (a b) -> p a b", a=2),
                                                    ACT.Copy), t, t_z, t_cv[j % 3])
            freed[i] = t1
            ts = []
            for m in range(2):
                n = j + 24 * m
                t2 = V(lambda e, m=m, n=n, u=u, w=w: e.tensor_scalar(w[:, m, :], u[:, m, 2:258], C("fw", 96 + n),
                                                                     C("fb", n), ALU.mult, ALU.add), t1, t_cv[j % 3])
                for k in (1, 0):
                    t2 = V(lambda e, m=m, n=n, u=u, w=w, k=k: e.scalar_tensor_tensor(
                        w[:, m, :], u[:, m, k:k + 256], C("fw", 48 * k + n), w[:, m, :], ALU.mult, ALU.add), t2)
                ts.append(t2)
            t3 = A(lambda e, w=w: e.activation(w[:, 0, :], w[:, 0, :], ACT.Gelu_apprx_tanh), ts[0])
            t_ff = V(lambda e, j=j, w=w: e.tensor_tensor(ff[:, j, :], w[:, 0, :], w[:, 1, :], ALU.mult), t3, ts[1])
            t_cv[j % 3] = t_ff
            some()
        while some():
            pass
        for g in range(3):
            t_m2 = ada(a["w_ada_2"], g, 1, "b_ada2", t_crep)

        sqs = W[0:2]
        sqrt_table()
        for c in range(4):
            i0, b0, f0 = bank()
            i1, b1_, f1 = bank()
            for kk in range(3):
                s, v, tl = load(a["down"][c, kk])
                for k in range(8):
                    for j, bb in ((0, b0), (1, b1_)):
                        t = T(lambda e, k=k, j=j, bb=bb, kk=kk, v=v: e.matmul(
                            bb[:, 0:256], v[:, k * 256 + j * 128:k * 256 + j * 128 + 128], ff[:, kk * 8 + k, :],
                            start=(kk == 0 and k == 0), stop=(kk == 2 and k == 7)), f0, f1, tl, t_ff,
                            inc=(k == 7 and j == 1))
                done(s, t)
            for j, bb in ((0, b0), (1, b1_)):
                n = 2 * c + j
                t5 = V(lambda e, n=n, bb=bb: e.scalar_tensor_tensor(xT[:, n, :], bb[:, 0:256],
                                                                    modc[:, 0, 40 + n:41 + n], xT[:, n, :],
                                                                    ALU.mult, ALU.add), t)
                freed[(i0, i1)[j]] = t5
            norm_square(c, sqs[c % 2], freed[i0], freed[i1], P.last("pe"))
            if c:
                norm_sum(c - 1)
        norm_sum(3)
        fence()

        t_r = norm_end(rst)
        t_h = modulate(1, 0, "pre_mix", rst, t_r, t_m2)

        cq, ckv = carve(2, 256), carve(256)
        qh, kh = carve(8, 256), carve(8, 256)
        vm, vd = carve(2, 512), carve(2, 128)
        qd, kd = carve(4, 256), carve(256)
        qi, ki = carve(2, 256), carve(256)
        widx = carve(2, 8)
        t_cs, t_dist = got["cs"], got["dist"]
        isc, selb = carve(384), carve(384)
        whole = carve(3072)
        W = [whole[:, 512 * n:512 * n + 512] for n in range(6)]
        HW = [whole[:, 384 * n:384 * n + 384] for n in range(8)]
        st = carve(96)
        m8 = carve(8)

        serial[0] = True

        def chunk2(n):
            s, v, tl = load(a["w2in"][n])
            i, b, fr = bank()
            t = tiles2(v, hT, [tl, t_h], b=b, fr=fr)
            done(s, t)
            return i, b, t

        i, b, t = chunk2(4)
        t_qi = A(lambda e: e.activation(qi.rearrange("p a b -> p (a b)"), b[:, :], ACT.Copy), t)
        freed[i] = t_qi
        i, b, t = chunk2(5)
        t1 = A(lambda e: e.activation(ki, b[:, 0:256], ACT.Copy), t)
        t_ki = A(lambda e: e.activation(kd, b[:, 256:512], ACT.Copy), t)
        freed[i] = t_ki
        s, v, tl = load(a["wv"], 8 * 136)
        i, b, fr = bank()
        for tt in range(2):
            for k in range(8):
                t = T(lambda e: e.matmul(b[:, 256 * tt:256 * tt + 136], hT[:, k, tt * 128:(tt + 1) * 128],
                                         v[:, k * 136:(k + 1) * 136], start=(k == 0), stop=(k == 7)),
                      fr, tl, t_h, inc=(tt == 1 and k == 7))
        done(s, t)
        bv = b[:, :].rearrange("p (a b) -> p a b", a=2)
        t_vd = A(lambda e: e.activation(vd, bv[:, :, 0:128], ACT.Copy), t)
        t_w = A(lambda e: e.activation(widx, bv[:, :, 128:136], ACT.Copy, scale=float(8 ** -0.5 * 32 ** -0.5)), t)
        freed[i] = t_w
        t_is = None
        for h in range(8):
            r, tq = 32 * (h % 4), h // 4
            i, b, fr = bank()
            T(lambda e: e.matmul(b[:, 0:128], qi[r:r + 32, tq, 0:128], ki[r:r + 32, 0:128], start=True, stop=True),
              fr, t_qi, t_ki)
            t = T(lambda e: e.matmul(b[:, 128:384], qi[r:r + 32, tq, 128:256], ki[r:r + 32, 0:256], start=True,
                                     stop=True), inc=True)
            dst = isc if h == 0 else W[4][:, 0:384]
            V(lambda e: e.tensor_scalar(dst[:, 0:128], b[:, 0:128], 0.0, widx[:, 0, h:h + 1], ALU.max, ALU.mult),
              t, t_w, t_is)
            t = V(lambda e: e.tensor_scalar(dst[:, 128:384], b[:, 128:384], 0.0, widx[:, 1, h:h + 1], ALU.max,
                                            ALU.mult))
            freed[i] = t
            if h:
                t_is = V(lambda e: e.tensor_tensor(isc, isc, dst, ALU.add), t, t_is)
            else:
                t_is = t
        t_is = V(lambda e: e.tensor_tensor(isc, isc, K("cbias"), ALU.add), t_is)

        def topk():
            for lo, hi in ((0, 128), (128, 384)):
                sv = isc[:, lo:hi]
                t = t_is
                for n in range(8):
                    t = V(lambda e: e.max(m8, sv), t)
                    t = V(lambda e: e.match_replace(sv, m8, sv, -3e38), t)
                    if n % 2:
                        yield
            t = V(lambda e: e.tensor_scalar(selb, isc, -2e38, NEG, ALU.is_gt, ALU.mult), t)
            got["sel"] = V(lambda e: e.tensor_tensor(selb, selb, K("cbias"), ALU.add), t)

        rounds = topk()

        i, b, t = chunk2(0)
        cqf = cq.rearrange("p a b -> p (a b)")
        t1 = V(lambda e: e.tensor_copy(cqf, b[:, :]), t)
        freed[i] = t1
        t2 = rms(cq, 2, 256, W[0].rearrange("p (a b) -> p a b", a=2), W[1][:, 0:256], 256, t1)
        for k in range(2):
            t_cq = V(lambda e: e.scalar_tensor_tensor(cq[:, k, :], cq[:, k, :], C("gq", k), W[1][:, 0:256], ALU.mult,
                                                      ALU.mult), t2)
        i, b, t = chunk2(1)
        t1 = V(lambda e: e.tensor_copy(ckv, b[:, 0:256]), t)
        t2 = V(lambda e: e.tensor_tensor(W[5][64:96, 0:256], b[64:96, 256:512], cs[64:96, :], ALU.mult), t, t_cs)
        t3 = V(lambda e: e.tensor_tensor(W[5][64:96, 256:512], b[96:128, 256:512], cs[96:128, :], ALU.mult), t)
        freed[i] = t3
        t3 = V(lambda e: e.tensor_tensor(W[5][64:96, 0:256], W[5][64:96, 0:256], W[5][64:96, 256:512], ALU.add),
               t2, t3)
        t_kr = V(lambda e: e.tensor_copy(kh[64:96, :, :],
                                         W[5][64:96, 0:256].unsqueeze(1).to_broadcast([32, 8, 256])), t3)
        t2 = rms(ckv, 1, 128, W[0][:, 0:256], W[1][:, 0:256], 256, t1, t_cq)
        t_ckv = V(lambda e: e.scalar_tensor_tensor(ckv, ckv, C("gkv"), W[1][:, 0:256], ALU.mult, ALU.mult), t2)
        for _ in range(8):
            next(rounds)
        for n in (2, 3):
            i, b, t = chunk2(n)
            t_qd = A(lambda e: e.activation(qd[:, 2 * n - 4:2 * n - 2, :].rearrange("p a b -> p (a b)"), b[:, :],
                                            ACT.Copy, scale=0.125), t)
            freed[i] = t_qd
        s, v, tl = load(a["qb"])
        t_qh = []
        for p in range(4):
            i, b, fr = bank()
            for j in range(2):
                for k in range(2):
                    h = 2 * p + j
                    t = T(lambda e: e.matmul(b[:, 256 * j:256 * j + 256],
                                             v[:, k * 1024 + h * 128:k * 1024 + h * 128 + 128], cq[:, k, :],
                                             start=(k == 0), stop=(k == 1)), fr, tl, t_cq, inc=(j == 1 and k == 1))
            bv = b[:, :].rearrange("p (a b) -> p a b", a=2)
            wv_ = W[4].rearrange("p (a b) -> p a b", a=2)
            t1 = A(lambda e: e.activation(qh[0:64, 2 * p:2 * p + 2, :], bv[0:64], ACT.Copy), t)
            t2 = V(lambda e: e.tensor_tensor(qh[64:96, 2 * p:2 * p + 2, :], bv[64:96],
                                             cs[64:96, :].unsqueeze(1).to_broadcast([32, 2, 256]), ALU.mult), t, t_cs)
            t3 = V(lambda e: e.tensor_tensor(wv_[64:96], bv[96:128],
                                             cs[96:128, :].unsqueeze(1).to_broadcast([32, 2, 256]), ALU.mult), t)
            freed[i] = [t1, t3]
            t3 = V(lambda e: e.tensor_tensor(qh[64:96, 2 * p:2 * p + 2, :], qh[64:96, 2 * p:2 * p + 2, :], wv_[64:96],
                                             ALU.add), t2, t3)
            t_qh += [t1, t3]
        done(s, t)
        s, v, tl = load(a["kvb"], 1024)
        for p in range(4):
            i, b, fr = bank()
            for j in range(2):
                h = 2 * p + j
                t = T(lambda e: e.matmul(b[0:64, 256 * j:256 * j + 256], v[:, h * 64:h * 64 + 64], ckv, start=True,
                                         stop=True), fr, tl, t_ckv, inc=(j == 1))
            t_kh = A(lambda e: e.activation(kh[0:64, 2 * p:2 * p + 2, :].rearrange("p a b -> p (a b)"), b[0:64, :],
                                            ACT.Copy), t)
            freed[i] = t_kh
        for tt in range(2):
            i, b, fr = bank()
            t = T(lambda e: e.matmul(b[:, :], ckv[:, tt * 128:(tt + 1) * 128], v[:, 512:1024], start=True, stop=True),
                  fr, inc=True)
            t_vm = A(lambda e: e.activation(vm[:, tt, :], b[:, :], ACT.Copy), t)
            freed[i] = t_vm
        done(s, t)
        fence_tokens = [P.last("dve"), P.last("act"), P.last("pe")]

        mix2 = hT
        heads, turned = {}, {}
        ybank = {}
        wfree = [None] * 4
        pfree = [None] * 4

        def head_scores(n):
            i, b, fr = bank()
            if n < 8:
                ks, qs = kh[0:96, n, :], qh[0:96, n, :]
                dep = [t_qh, t_kh, t_kr]
            else:
                h = n - 8
                r = 64 * (h // 4)
                ks, qs = kd[r:r + 64, :], qd[r:r + 64, h % 4, :]
                dep = [t_qd, t_ki]
            T(lambda e: e.matmul(b[:, 0:128], qs[:, 0:128], ks[:, 0:128], start=True, stop=True), fr, dep)
            t = T(lambda e: e.matmul(b[:, 128:384], qs[:, 128:256], ks[:, 0:256], start=True, stop=True), inc=True)
            w = HW[n % 4]
            so = st[:, 6 * n:6 * n + 6]
            if n < 8:
                t = V(lambda e: e.scalar_tensor_tensor(w, b[:, 0:384], float(96 ** -0.5), K("cbias"), ALU.mult,
                                                       ALU.add), t, wfree[n % 4], fence_tokens)
                freed[i] = t
            else:
                slope = float(2.0 ** -(n - 8 + 1))
                t = V(lambda e: e.scalar_tensor_tensor(w, dist, -slope, b[:, 0:384], ALU.mult, ALU.add), t,
                      wfree[n % 4], fence_tokens, t_dist)
                freed[i] = t
                t = V(lambda e: e.tensor_tensor(w, w, selb, ALU.add), t, got["sel"])
            seg = ((0, 0, 128), (1, 128, 384))
            for tt, lo, hi in seg:
                t1 = V(lambda e: e.tensor_reduce(so[:, tt:tt + 1], w[:, lo:hi], AX.X, ALU.max, negate=True), t)
            for tt, lo, hi in seg:
                t2 = A(lambda e: e.activation(w[:, lo:hi], w[:, lo:hi], ACT.Exp, bias=so[:, tt:tt + 1],
                                              accum_out=so[:, 2 + tt:3 + tt]), t1)
            heads[n] = t2

        def head_weights(n):
            w = HW[n % 4]
            so = st[:, 6 * n:6 * n + 6]
            t3 = V(lambda e: e.reciprocal(so[:, 4:6], so[:, 2:4]), heads[n])
            for tt, lo, hi in ((0, 0, 128), (1, 128, 384)):
                t3_ = V(lambda e: e.tensor_scalar(w[:, lo:hi], w[:, lo:hi], so[:, 4 + tt:5 + tt], None, ALU.mult), t3)
            heads[n] = t3_

        def head_turn(n):
            w = HW[n % 4]
            pt = HW[4 + n % 4]
            i, b, fr = bank()
            for q in range(3):
                t = T(lambda e: e.transpose(b[:, 128 * q:128 * q + 128], w[:, 128 * q:128 * q + 128], K("ident")),
                      fr, heads[n], inc=(q == 2))
            wfree[n % 4] = t
            t = A(lambda e: e.activation(pt, b[:, 0:384], ACT.Copy), t, pfree[n % 4], fence_tokens)
            freed[i] = t
            turned[n] = t

        def head_out(n):
            pt, t = HW[4 + n % 4], turned[n]
            if n % 2 == 0:
                ybank[n // 2] = bank()
            iy, by, fr = ybank[n // 2]
            r = 64 * (n % 2)
            if n < 8:
                v0, v1 = vm[:, 0, n * 64:n * 64 + 64], vm[:, 1, n * 64:n * 64 + 64]
            else:
                o0 = 64 * ((n - 8) // 4)
                v0, v1 = vd[:, 0, o0:o0 + 64], vd[:, 1, o0:o0 + 64]
            T(lambda e: e.matmul(by[r:r + 64, 0:256], v0, pt[:, 0:256], start=True, stop=False,
                                 skip_group_check=True), fr, t, t_vm, t_vd)
            t = T(lambda e: e.matmul(by[r:r + 64, 128:256], v1, pt[:, 256:384], start=False, stop=True,
                                     skip_group_check=True), inc=True)
            pfree[n % 4] = t
            if n % 2:
                t1 = V(lambda e: e.tensor_copy(mix2[:, n // 2, :], by[:, 0:256]), t)
                freed[iy] = t1
                heads[n] = t1

        for n in range(19):
            if n >= 3:
                head_turn(n - 3)
            if n < 16:
                head_scores(n)
            if 1 <= n < 17:
                head_weights(n - 1)
            if n < 8:
                next(rounds, None)
                if n == 7:
                    next(rounds, None)
            if n >= 3:
                head_out(n - 3)
        t_mx = [heads[n] for n in range(1, 16, 2)]

        mo = qh
        sq = kh
        t1 = V(lambda e: e.tensor_tensor(mc[:, 8:16], modc[:, 1, 16:24], C("post_mix", 0, 8), ALU.mult))
        sqrt_table()
        for c in range(4):
            s, v, tl = load(a["w_o"][c])
            i, b, fr = bank()
            t = tiles2(v, mix2, [tl, t_mx], b=b, fr=fr)
            done(s, t)
            sqc = sq[:, 2 * c:2 * c + 2, :].rearrange("p a b -> p (a b)")
            norm[c] = (sqc, A(lambda e: e.activation(sqc, b[:, :], ACT.Square), t))
            for j in range(2):
                t_mo = V(lambda e: e.tensor_scalar(mo[:, 2 * c + j, :], b[:, 256 * j:256 * j + 256],
                                                   mc[:, 8 + 2 * c + j:9 + 2 * c + j], None, ALU.mult), norm[c][1], t1)
            freed[i] = [t_mo, norm[c][1]]
            if c:
                norm_sum(c - 1)
        norm_sum(3)
        t_r = norm_end(W[0][:, 0:256])
        for c in range(4):
            two = slice(2 * c, 2 * c + 2)
            V(lambda e: e.tensor_tensor(mo[:, two, :], mo[:, two, :],
                                        W[0][:, 0:256].unsqueeze(1).to_broadcast([128, 2, 256]), ALU.mult), t_r)
            t_x = V(lambda e: e.tensor_tensor(xT[:, two, :], xT[:, two, :], mo[:, two, :], ALU.add))
            norm_square(c, sq[:, two, :].rearrange("p a b -> p (a b)"), t_x, P.last("pe"))
            norm_sum(c)
        fence()
        h4 = carve(2, 1024)
        acc = carve(2, 1024)
        V(lambda e: e.memset(acc, 0.0))
        t_r = norm_end(rst)
        t_h = modulate(1, 3, "pre_ffn", rst, t_r)

        top[0] += 640
        lg, mk, gt, posm = carve(2, 32), carve(2, 32), carve(2, 32), carve(2, 32)
        tmp = [carve(2, 32) for _ in range(3)]
        sm = carve(32)
        mm8 = carve(2, 8)
        zer = carve(32)
        cntf = carve(32)
        gT = carve(2, 128)
        xe_all = carve(2, 1024)
        xe = [[xe_all[:, c, 512 * n:512 * n + 512] for n in range(2)] for c in range(2)]
        selT = [carve(256), carve(256)]
        pairT = [[carve(256), carve(256)] for _ in range(2)]
        xg = carve(512)
        sel = [carve(2, 64) for _ in range(2)]
        selg = [carve(2, 128) for _ in range(2)]
        w0, w1, w2 = [carve(512) for _ in range(3)]
        actb = [w0, carve(512)]
        t_b1 = got["b1"]
        cnti = sb("cnti", [128, 33], I32)

        b2 = carve(1024)[0:32]
        P.dma("act", lambda e: e.dma_start(b2, a["b2"]), s_p[4])
        t_z = V(lambda e: e.memset(zer, 0.0))
        s_wr, v, tl = load(a["wr"], 256)
        i, b, fr = bank()
        for k in range(8):
            t = T(lambda e: e.matmul(b[0:32, 0:256], v[:, k * 32:(k + 1) * 32], hT[:, k, :], start=(k == 0),
                                     stop=(k == 7)), fr, tl, t_h[k], inc=(k == 7))
        done(s_wr, t)
        gTf = gT[0:32].rearrange("p a b -> p (a b)")
        t = A(lambda e: e.activation(gTf, b[0:32, 0:256], ACT.Copy), t)
        freed[i] = t
        A(lambda e: e.activation(onec[:, 1:2], eps[:, 0:1], ACT.Exp), t_h)
        i, b, fr = bank()
        for tt in range(2):
            t = T(lambda e: e.transpose(b[:, 32 * tt:32 * tt + 32], gTf[:, 128 * tt:128 * tt + 128],
                                        K("ident", 0, 32)[0:32, :]), fr, t, inc=(tt == 1))
        t_lg = V(lambda e: e.tensor_tensor(lg, b[:, 0:64].rearrange("p (a b) -> p a b", a=2),
                                           brt[:, :].unsqueeze(1).to_broadcast([128, 2, 32]), ALU.add),
                 t, (s_p[2], 16))
        freed[i] = t_lg
        t_lt = t
        for tt in range(2):
            for q in range(2):
                i, b, fr = bank()
                for k in range(4):
                    t = T(lambda e: e.transpose(b[:, 128 * k:128 * k + 128],
                                                hT[:, 4 * q + k, tt * 128:(tt + 1) * 128], K("ident")), fr,
                          inc=(k == 3))
                t_h4 = A(lambda e: e.activation(h4[:, tt, q * 512:(q + 1) * 512], b[:, :], ACT.Copy), t)
                freed[i] = t_h4
        gtt, cum, eq = tmp
        so = sm.rearrange("p (a b) -> p a b", a=2)

        def wide(v):
            return v.to_broadcast([128, 2, 32])

        for tt in range(2):
            V(lambda e: e.max(mm8[:, tt, :], lg[:, tt, :]))
        v4 = wide(mm8[:, :, 3:4])
        t1 = V(lambda e: e.tensor_tensor(cum, lg, wide(mm8[:, :, 0:1]), ALU.subtract))
        t_e = A(lambda e: e.activation(gt, cum, ACT.Exp), t1)
        V(lambda e: e.tensor_tensor(gtt, lg, v4, ALU.is_gt))
        V(lambda e: e.tensor_tensor(eq, lg, v4, ALU.is_equal))
        V(lambda e: e.tensor_reduce(so[:, :, 0:1], gtt, AX.X, ALU.add))
        for tt in range(2):
            V(lambda e: e.tensor_tensor_scan(cum[:, tt, :], eq[:, tt, :], zer, 0.0, ALU.add, ALU.add), t_z, t_e)
        V(lambda e: e.tensor_scalar(so[:, :, 1:2], so[:, :, 0:1], -1.0, 4.0, ALU.mult, ALU.add))
        V(lambda e: e.tensor_tensor(cum, cum, wide(so[:, :, 1:2]), ALU.is_le))
        V(lambda e: e.tensor_tensor(eq, eq, cum, ALU.mult))
        t_mk = V(lambda e: e.tensor_tensor(mk, gtt, eq, ALU.add))
        V(lambda e: e.tensor_tensor(gt, gt, mk, ALU.mult), t_e)
        V(lambda e: e.tensor_reduce(so[:, :, 3:4], gt, AX.X, ALU.add))
        V(lambda e: e.reciprocal(so[:, :, 4:5], so[:, :, 3:4]))
        t_g = V(lambda e: e.tensor_tensor(gt, gt, wide(so[:, :, 4:5]), ALU.mult))
        i, b, fr = bank()
        T(lambda e: e.matmul(b[:, 0:32], K("uinc"), mk[:, 0, :], start=True, stop=True), fr, t_mk)
        T(lambda e: e.matmul(b[:, 32:64], K("ones"), mk[:, 0, :], start=True, stop=False))
        T(lambda e: e.matmul(b[:, 32:64], K("uinc"), mk[:, 1, :], start=False, stop=True))
        T(lambda e: e.matmul(b[:, 64:96], K("ones"), mk[:, 0, :], start=True, stop=False))
        t = T(lambda e: e.matmul(b[:, 64:96], K("ones"), mk[:, 1, :], start=False, stop=True), inc=True)
        V(lambda e: e.tensor_copy(cntf, b[:, 64:96]), t)
        t_ci = V(lambda e: e.tensor_copy(cnti[:, 0:32], cntf))
        t_ci = V(lambda e: e.tensor_reduce(cnti[:, 32:33], cntf, AX.X, ALU.max))
        t1 = V(lambda e: e.tensor_tensor(posm, b[:, 0:64].rearrange("p (a b) -> p a b", a=2), mk, ALU.mult))
        freed[i] = t1
        t_pos = V(lambda e: e.tensor_scalar(posm, posm, -1.0, None, ALU.add))
        i, b, fr = bank()
        for tt in range(2):
            t = T(lambda e: e.transpose(b[0:32, 128 * tt:128 * tt + 128], gt[:, tt, :], K("ident")), fr, t_g,
                  inc=True)
        t = V(lambda e: e.tensor_copy(gTf, b[0:32, 0:256]), t, t_lt)
        freed[i] = t
        fence_tokens = [P.last(e) for e in ("pe", "act", "dve")]
        for e_ in ("pe", "act", "dve"):
            P.wait(e_, fence_tokens)
            P.wait(e_, t_ci, t_b1, t_s96, t_pos, t_g, (s_p[4], 16))
        serial[0] = False
        HID = [[B[0], B[1]], [B[2], B[3]]]
        OUT = [[B[4], B[5]], [B[6], B[7]]]
        spare = hT[:, :, :].rearrange("p a b -> p (a b)")
        aT = [spare[:, 0:512], spare[:, 512:1024]]
        ypair = [spare[:, 1024:1536], spare[:, 1536:2048]]
        ysb = carve(512)
        tok = {}

        def places(x, c):
            io = K("iota", 128 * c, 128 * c + 128)
            for tt in range(2):
                t_s = V(lambda e: e.tensor_scalar(sel[c][:, tt, :], io[:, 0:64], posm[:, tt, x:x + 1], None,
                                                  ALU.is_equal), tok.get(("sel", c)))
            for tt in range(2):
                t_sg = V(lambda e: e.tensor_scalar(selg[c][:, tt, :], io, posm[:, tt, x:x + 1],
                                                   gt[:, tt, x:x + 1], ALU.is_equal, ALU.mult), tok.get(("selg", c)))
            return t_s, t_sg

        def gather(x, c, t_s, t_sg):
            for tt in range(2):
                for hf in range(2):
                    t = T(lambda e: e.matmul(B[3][64 * hf:64 * hf + 64, :], sel[c][:, tt, :],
                                             h4[:, tt, hf * 512:(hf + 1) * 512], start=(tt == 0), stop=(tt == 1),
                                             skip_group_check=True), t_s, freed[3], inc=(tt == 1 and hf == 1))
            tok["sel", c] = t
            t_xg = A(lambda e: e.activation(xg, B[3][:, :], ACT.Copy), t, tok.get("xg"))
            for tt in range(2):
                t = T(lambda e: e.transpose(B[2][:, 128 * tt:128 * tt + 128], selg[c][:, tt, :], K("ident")), t_sg,
                      freed[2], inc=(tt == 1))
            tok["selg", c] = t
            if c:
                t_sT = V(lambda e: e.tensor_copy(selT[x % 2], B[2][:, 0:256]), t, tok.get(("selT", x % 2)))
            else:
                for g in range(2):
                    rows = slice(64 * g, 64 * g + 64)
                    t_sT = V(lambda e: e.tensor_copy(pairT[x // 2 % 2][g ^ x % 2][rows, :], B[2][rows, 0:256]), t,
                             tok.get(("pairT", x // 2 % 2)))
            freed[2] = t_sT
            return t_xg, t_sT

        def gather_turn(x, c, t_xg, t_sT):
            xb = xe[c][x % 2]
            for q in range(4):
                t = T(lambda e: e.transpose(B[3][:, 128 * q:128 * q + 128], xg[:, 128 * q:128 * q + 128],
                                            K("ident")), t_xg, inc=(q == 3))
            tok["xg"] = t
            t_xe = A(lambda e: e.activation(xb, B[3][:, :], ACT.Copy), t, tok.get(("xe", c, x % 2)))
            freed[3] = t_xe
            tok["gathered", c, x] = (t_xe, t_sT)

        def up(x, cs, pieces_):
            for c in cs:
                for n in range(2):
                    for hf in range(2):
                        o0 = hf * 1024 + n * 512
                        T(lambda e: e.matmul(HID[c][n][64 * hf:64 * hf + 64, :], sel96[:, x:x + 1].to_broadcast([96, 64]),
                                             b1h[:, o0:o0 + 512], start=True, stop=False, skip_group_check=True),
                          [freed[0], freed[1]] if c == 0 else [freed[2], freed[3]])
            o = []
            for k in range(8):
                s, v, tl = pieces_[k]
                xo = 128 * (k % 4) + 64 * (k // 4)
                for c in cs:
                    for n in range(2):
                        for hf in range(2):
                            o0 = hf * 1024 + n * 512
                            t = T(lambda e: e.matmul(HID[c][n][64 * hf:64 * hf + 64, :],
                                                     xe[c][x % 2][:, xo:xo + 64], v[:, o0:o0 + 512], start=False,
                                                     stop=(k == 7), skip_group_check=True),
                                  tl, tok["gathered", c, x][0],
                                  inc=(hf == 1 and (c == cs[-1] and n == 1 or k == 7 and c == n == 0)))
                            if k == 7 and c == n == 0 and hf == 1:
                                first = t
                o.append(t)
            o.append(first)
            return o

        def act(c, tn):
            ts = []
            for n in range(2):
                t = tn[n]
                hv = HID[c][n][:, :].rearrange("p (f two) -> p f two", two=2)
                sl = slice(256 * n, 256 * n + 256)
                tg = V(lambda e: e.tensor_scalar(actb[c][:, sl], hv[:, :, 0], 7.0, None, ALU.min), t,
                       tok.get(("actb", c)), tok.get("w"))
                tl2 = V(lambda e: e.tensor_scalar(w1[:, sl], hv[:, :, 1], -7.0, 7.0, ALU.max, ALU.min), t)
                tsg = A(lambda e: e.activation(w2[:, sl], actb[c][:, sl], ACT.Sigmoid, scale=1.702), tg, tok.get("w"))
                t3 = V(lambda e: e.scalar_tensor_tensor(w1[:, sl], w1[:, sl], 1.0, actb[c][:, sl], ALU.add,
                                                        ALU.mult), tg, tl2)
                freed[2 * c + n] = tl2
                ts.append((sl, t3, tsg))
            o = [V(lambda e: e.tensor_tensor(actb[c][:, sl], w1[:, sl], w2[:, sl], ALU.mult), t3, tsg)
                 for sl, t3, tsg in ts]
            tok["w"] = o
            return o

        def turn_act(c, ts):
            for q in range(4):
                t = T(lambda e: e.transpose(B[c][:, 128 * q:128 * q + 128], actb[c][:, 128 * q:128 * q + 128],
                                            K("ident")), freed[c], ts[q // 2], inc=(q == 3))
            tok["actb", c] = t
            t = A(lambda e: e.activation(aT[c], B[c][:, :], ACT.Copy), t, tok.get(("aT", c)))
            freed[c] = t
            return t

        def down(x, cs, ta, pieces_):
            o = []
            for kt in range(8):
                s, v, tl = pieces_[kt // 2]
                q, hf = kt % 4, kt // 4
                for c in cs:
                    for oh in range(2):
                        g = 64 * (oh if c else oh ^ x % 2)
                        t = T(lambda e: e.matmul(B[2 + c][g:g + 64, :],
                                                 aT[c][:, 128 * q + 64 * hf:128 * q + 64 * hf + 64],
                                                 v[:, (kt % 2) * 1024 + oh * 512:(kt % 2) * 1024 + oh * 512 + 512],
                                                 start=(kt == 0), stop=(kt == 7), skip_group_check=True), ta[c], tl,
                              freed[2 + c] if kt == 0 else None, inc=(kt % 2 == 1 and c == cs[-1] and oh == 1))
                if kt % 2:
                    o.append(t)
            if 1 in cs:
                ty = A(lambda e: e.activation(ysb, B[3][:, :], ACT.Copy), o[-1], tok.get("ysb"))
                freed[3] = ty
                for tt in range(2):
                    for oh in range(2):
                        t = T(lambda e: e.matmul(OUT[tt][oh][:, :],
                                                 selT[x % 2][64 * oh:64 * oh + 64, tt * 128:(tt + 1) * 128],
                                                 ysb[64 * oh:64 * oh + 64, :], start=False, stop=False,
                                                 skip_group_check=True), ty, tok["gathered", 1, x][1],
                              inc=(tt == 1 and oh == 1))
            return o

        def to_pair(x):
            r0, r1 = slice(0, 64), slice(64, 128)
            w = [P.last("pe"), tok.get("ypair")]
            t0 = A(lambda e: e.activation(ypair[x % 2][r0, :], B[2][r0, :], ACT.Copy), w)
            t1 = V(lambda e: e.tensor_copy(ypair[1 - x % 2][r1, :], B[2][r1, :]), w)
            freed[2] = [t0, t1]
            tok["y", x % 2] = [t0, t1]

        def add_pair(x):
            o = []
            for tt in range(2):
                for oh in range(2):
                    t = T(lambda e: e.matmul(OUT[tt][oh][:, :],
                                             pairT[x // 2 % 2][oh][:, tt * 128:(tt + 1) * 128], ypair[oh],
                                             start=False, stop=False, skip_group_check=True),
                          tok["y", 0], tok["y", 1], tok["gathered", 0, x - 1][1], tok["gathered", 0, x][1],
                          inc=(oh == 1))
                o.append(t)
            tok["ypair"] = tok["pairT", x // 2 % 2] = t
            return o

        w1_v = a["w_mlp1"].rearrange("x (k p) n -> x k p n", p=128)
        w2_v = a["w_mlp2"].rearrange("x (m k p) n -> x m p k n", p=128, k=2)
        plan = []
        for x in range(NE):
            plan += [(w1_v[x, k], 1) for k in range(8)] + [(w2_v[x, m], 2) for m in range(4)]
        phase_sems = [sem(f"wl{n}") for n in range(RING)]
        slot_sem[:] = phase_sems
        slot_use[:] = [0] * RING
        again = []
        ahead = []
        for src, _ in plan[:RING]:
            s = piece[0] % RING
            ahead.append(load(src))
            again.append((slot_view(s, src, SLOT), src, phase_sems[s]))
        P.wait("sp", t_ci)
        P.new_semaphores("_l")
        engines = ("pe", "act", "dve", "sp")

        def rest(e):
            return e.value_load(cnti[0:1, 32:33], min_val=-1000, max_val=256)

        P.begin_loop(engines, rest)
        for n in range(8):
            freed[n] = None
        nload = [RING]

        def next_pieces(n):
            o = []
            while len(queue) < n:
                queue.append(load(plan[nload[0]][0]))
                nload[0] += 1
            for _ in range(n):
                o.append(queue.pop(0))
            return o

        queue = list(ahead)
        for s, _, _ in ahead:
            slot_free[s] = False
        many = {}

        def count(x):
            for me_ in ("pe", "act", "dve"):
                if P.me == me_:
                    many[x] = P.eng.value_load(cnti[0:1, x:x + 1], min_val=-1000, max_val=256) > CAP
            many.setdefault(x)

        def keep():
            return dict(freed), dict(tok)

        def back(kept):
            freed.update(kept[0])
            tok.clear()
            tok.update(kept[1])

        def second(x):
            P.begin_if(("pe", "act", "dve"), many[x])
            gather_turn(x, 1, *gather(x, 1, *places(x, 1)))
            P.end_if()

        count(0)
        gather_turn(0, 0, *gather(0, 0, *places(0, 0)))
        second(0)
        for x in range(NE):
            if x + 1 < NE:
                nxt = places(x + 1, 0)
            p1 = next_pieces(8)
            P.begin_if(("pe",), many[x])
            tk = up(x, (0, 1), p1)
            P.begin_else()
            up(x, (0,), p1)
            P.end_if()
            for (s, _, _), t in zip(p1, tk):
                done(s, t)
            tok["xe", 0, x % 2] = tok["xe", 1, x % 2] = tk[7]
            ts = act(0, (tk[8], tk[7]))
            if x == NE - 1:
                serial[0] = True
                V(lambda e: e.memset(gT, 0.0), P.last("pe"), P.last("act"))
                V(lambda e: e.tensor_scalar(posm, posm, -2.0 * CAP, None, ALU.add))
                V(lambda e: e.tensor_scalar(cntf, cntf, -2.0 * CAP, None, ALU.add))
                V(lambda e: e.tensor_copy(cnti[:, 0:32], cntf))
                V(lambda e: e.tensor_reduce(cnti[:, 32:33], cntf, AX.X, ALU.max))
                serial[0] = False
            kept = keep()
            P.begin_if(("pe", "act", "dve"), many[x])
            ts1 = act(1, (tk[7], tk[7]))
            if x + 1 < NE:
                gather(x + 1, 0, *nxt)
                P.begin_else()
                back(kept)
                gather(x + 1, 0, *nxt)
            P.end_if()
            if x + 1 < NE:
                freed[2], freed[3] = P.last("dve"), P.last("act")
                tok["sel", 0] = tok["selg", 0] = P.last("pe")
                gathered = P.last("act"), P.last("dve")
                count(x + 1)
            if x == 0:
                for tt in range(2):
                    for oh in range(2):
                        T(lambda e: e.matmul(OUT[tt][oh][:, :], gT[0:32, tt, :], b2[:, oh * 512:(oh + 1) * 512],
                                             start=True, stop=False, skip_group_check=True))
            elif x % 2 == 0:
                add_pair(x - 1)
            ta = {0: turn_act(0, ts)}
            if x + 1 < NE:
                gather_turn(x + 1, 0, *gathered)
                second(x + 1)
            p2 = next_pieces(4)
            kept = keep()
            P.begin_if(("pe", "act"), many[x])
            ta[1] = turn_act(1, ts1)
            td = down(x, (0, 1), ta, p2)
            P.begin_else()
            back(kept)
            down(x, (0,), ta, p2)
            P.end_if()
            for (s, _, _), t in zip(p2, td):
                done(s, t)
            for n in (0, 1, 3):
                freed[n] = P.last("act")
            tok["ysb"] = tok["selT", x % 2] = P.last("pe")
            for c in (0, 1):
                tok["aT", c] = tok["actb", c] = P.last("pe")
            to_pair(x)
        t_out = add_pair(NE - 1)
        serial[0] = True
        A(lambda e: e.activation(onec[:, 1:2], eps[:, 0:1], ACT.Sqrt), P.last("act"))
        for tt in range(2):
            for q in range(2):
                V(lambda e: e.tensor_tensor(acc[:, tt, q * 512:(q + 1) * 512], OUT[tt][q][:, :],
                                            acc[:, tt, q * 512:(q + 1) * 512], ALU.add), t_out[tt])
            A(lambda e: e.activation(xe_all[:, tt, :], acc[:, tt, :], ACT.Square, accum_out=sm[:, tt:tt + 1]),
              P.last("dve"), P.last("act"))
        clear = [P.sem[e] for e in ("pe", "act", "dve")] + phase_sems
        go = {e: sem("go_" + e) for e in ("pe", "act", "dve")}
        P.end_loop(rest, clear, sem("bar"), go, again)

        ss = sm
        t = A(lambda e: e.activation(ss[:, 2:4], ss[:, 0:2], ACT.Sqrt, bias=eps[:, 0:1], scale=1.0 / D))
        t_c1 = V(lambda e: e.tensor_tensor(mc[:, 0:8], modc[:, 1, 40:48], C("post_ffn", 0, 8), ALU.mult))
        t = V(lambda e: e.reciprocal(ss[:, 4:6], ss[:, 2:4]), t)
        t_f = [V(lambda e: e.tensor_scalar(acc[:, 0, :], acc[:, 0, :], ss[:, 4:5], None, ALU.mult), t),
               A(lambda e: e.activation(acc[:, 1, :], acc[:, 1, :], ACT.Identity, scale=ss[:, 5:6]), t)]
        for n in (4, 5, 6, 7):
            freed[n] = t_f
        for n in (0, 1, 2, 3):
            freed[n] = None
        s_out = sem("s_out")
        for c in range(4):
            i, b, fr = bank()
            for j in range(2):
                for tt in range(2):
                    t = T(lambda e: e.transpose(b[:, 256 * j + 128 * tt:256 * j + 128 * tt + 128],
                                                acc[:, tt, (2 * c + j) * 128:(2 * c + j + 1) * 128], K("ident")), fr,
                          t_f, inc=(j == 1 and tt == 1))
            for j in range(2):
                n = 2 * c + j
                t_x = V(lambda e: e.scalar_tensor_tensor(xT[:, n, :], b[:, 256 * j:256 * j + 256], mc[:, n:n + 1],
                                                         xT[:, n, :], ALU.mult, ALU.add), t, t_c1)
            P.dma("sp", lambda e: e.dma_start(out[:, 2 * c:2 * c + 2, :], xT[:, 2 * c:2 * c + 2, :]), s_out, t_x)
        P.wait("sp", (s_out, 64))



def lay_out(i):
    def np_(n):
        return np.asarray(i[n])

    def cols(n):
        return np_(n).reshape(-1, 128).T

    def pieces(w, width=256):
        k, n = w.shape
        return np.ascontiguousarray(w.reshape(k // 128, 128, n // width, width).transpose(2, 1, 0, 3)).reshape(
            n // width, 128, k // 128 * width)

    o = {}
    o["xT"] = np.ascontiguousarray(np_("x")[0].T.reshape(8, 128, 256).transpose(1, 0, 2))
    order = ["c", "c_2", "ada_b", "b_ada_2", "norm1_g", "norm2_g", "conv_w", "conv_b", "rg_ba", "rg_bx", "rg_lambda",
             "q_norm_g", "k_norm_g", "ffn_conv_w", "ffn_conv_b", "g_pre_mix_2", "g_post_mix_2", "g_pre_ffn_2",
             "g_post_ffn_2", "g_q_a_2", "g_kv_a_2"]
    o["cols"] = np.ascontiguousarray(np.concatenate([cols(n) for n in order], 1))
    o["consts"] = constants()
    o["ada_w"] = np_("ada_w")[0]
    o["w_ada_2"] = np_("w_ada_2")[0]
    o["w_in"] = pieces(np_("w_in")[0])
    rg = np.stack([np_("rg_wa")[0], np_("rg_wx")[0]]).reshape(2, 4, 2, 128, 128)
    o["rg"] = np.ascontiguousarray(rg.transpose(1, 3, 0, 2, 4)).reshape(4, 128, 512)
    o["w_out"] = pieces(np_("w_out")[0])
    up = np_("ffn_up")[0].reshape(8, 128, 2, 24, 128)
    o["up"] = np.ascontiguousarray(up.transpose(3, 1, 0, 2, 4)).reshape(24, 128, 2048)
    dn = np_("ffn_down")[0].reshape(3, 8, 128, 4, 256)
    o["down"] = np.ascontiguousarray(dn.transpose(3, 0, 2, 1, 4)).reshape(4, 3, 128, 2048)
    w = np_("w_in_2")[0]
    cq, ckv, kr, qd, kd, vd, qi, ki, wi = np.split(w, np.cumsum([256, 128, 32, 512, 128, 128, 256, 32])[:8], axis=1)
    sw = np.concatenate([kr[:, 16:], kr[:, :16]], 1)
    qd = qd.reshape(1024, 2, 4, 64).transpose(0, 2, 1, 3).reshape(1024, 512)
    allc = np.concatenate([cq, ckv, kr, sw, kr, sw, qd, qi, ki, ki, ki, ki, kd], 1)
    o["w2in"] = pieces(allc)
    o["wv"] = pieces(np.concatenate([vd, wi], 1), 136)[0]
    qb = np_("w_q_b_2")[0].reshape(256, 8, 96)
    qb = np.concatenate([qb, qb[:, :, 80:96], qb[:, :, 64:80]], 2).reshape(256, 1024)
    o["qb"] = pieces(qb, 1024)[0]
    kvb = np_("w_kv_b_2")[0].reshape(128, 8, 2, 64).transpose(0, 2, 1, 3)
    o["kvb"] = np.ascontiguousarray(kvb).reshape(128, 1024)
    o["w_o"] = pieces(np_("w_o_2")[0])
    pos = np_("positions_2")[0]
    o["posr"] = np.ascontiguousarray(np.broadcast_to(pos[None], (128, 256)))
    o["posc"] = np.ascontiguousarray(pos.reshape(2, 128).T)
    o["wr"] = pieces(np_("w_router_2")[0], 32)[0]
    o["br"] = np.ascontiguousarray(np.broadcast_to(np_("b_router_2")[0][None], (128, 32)))
    o["b1"] = np.concatenate([np_("b_mlp1_2")[0]] * 3, 0)
    o["b2"] = np_("b_mlp2_2")[0]
    r = np.arange(96)[:, None] % 32 == np.arange(NE)[None, :]
    o["sel96"] = (r * 0x3F80).astype(np.uint16).view(np.float32)
    o["w_mlp1"] = np_("w_mlp1_2")[0]
    o["w_mlp2"] = np_("w_mlp2_2")[0]
    return o


def kernel(**inputs):
    import concourse.bacc as bacc
    from concourse.bass_utils import run_bass_kernel_spmd as launch

    nc = bacc.Bacc("TRN2", target_bir_lowering=False, num_devices=1, dynamic_dma_scratch_size=256)
    arrays, aps = {}, {}
    for name, v in lay_out(inputs).items():
        arrays["in_" + name] = v
        aps[name] = nc.dram_tensor("in_" + name, v.shape, mybir.dt.from_np(v.dtype), kind="ExternalInput").ap()
    o = nc.dram_tensor("out_xT", (128, 8, 256), F32, kind="ExternalOutput").ap()
    program(nc, aps, o)
    r = launch(nc, [arrays], core_ids=[0])
    y = r.results[0]["out_xT"]
    return np.ascontiguousarray(y.transpose(1, 0, 2).reshape(1024, 256).T)[None]
```
